# Optimizing a Trainium2 kernel written in Bass

```python
import math
import jax, jax.numpy as jnp
from jax import lax
import numpy as np

D_MODEL = 1024
BATCH = 1
SEQ = 256
DEPTH = 1

RNN_WIDTH = 1024
RNN_BLOCKS = 16
RNN_BLOCK_DIM = RNN_WIDTH // RNN_BLOCKS
CONV_WIDTH = 4
LRU_C = 8.0
N_HEADS = 8
HEAD_DIM = 128
ATTN_WIDTH = N_HEADS * HEAD_DIM
ROPE_DIM = HEAD_DIM // 4
ROPE_THETA = 500000.0
MOBA_BLOCK = 256
MOBA_TOPK = 3
Q_CHUNK = 256
N_EXPERTS = 32
TOP_K = 4
D_EXPERT = 1024
SWIGLU_LIMIT = 7.0
SWIGLU_ALPHA = 1.702
EXPERT_ROWS = 256
EPS = 1e-6
NEG = -1e30

kernel_name = 'hybrid_rglru_moba_moe'

def rms_norm(x, g):
    xf = x.astype(jnp.float32)
    y = xf * lax.rsqrt(jnp.mean(xf * xf, axis=-1, keepdims=True) + EPS)
    return (y * g.astype(jnp.float32)).astype(x.dtype)

def causal_depthwise_conv(x, w, b):
    s = x.shape[1]
    xp = jnp.pad(x, ((0, 0), (CONV_WIDTH - 1, 0), (0, 0)))
    y = b
    for tap in range(CONV_WIDTH):
        y = y + xp[:, tap:tap + s] * w[tap]
    return y

def rg_lru(x, wx, bx, wa, ba, a_param):
    bsz, s, c = x.shape
    xb = x.reshape(bsz, s, RNN_BLOCKS, RNN_BLOCK_DIM)
    gate_x = jax.nn.sigmoid(jnp.einsum('bsgi,gij->bsgj', xb, wx).reshape(bsz, s, c) + bx)
    gate_a = jax.nn.sigmoid(jnp.einsum('bsgi,gij->bsgj', xb, wa).reshape(bsz, s, c) + ba)
    log_a = -LRU_C * gate_a.astype(jnp.float32) * jax.nn.softplus(-a_param.astype(jnp.float32))
    a = jnp.exp(log_a)
    u = jnp.sqrt(-jnp.expm1(2.0 * log_a)) * (gate_x * x).astype(jnp.float32)

    def combine(left, right):
        a_l, b_l = left
        a_r, b_r = right
        return a_l * a_r, a_r * b_l + b_r

    _, h = lax.associative_scan(combine, (a, u), axis=1)
    return h.astype(x.dtype)

def partial_rotary(x):
    s = x.shape[1]
    half = ROPE_DIM // 2
    inv_freq = ROPE_THETA ** (-jnp.arange(half, dtype=jnp.float32) * (2.0 / ROPE_DIM))
    ang = jnp.arange(s, dtype=jnp.float32)[:, None] * inv_freq[None, :]
    cos = jnp.cos(ang)[:, None, :]
    sin = jnp.sin(ang)[:, None, :]
    xf = x.astype(jnp.float32)
    x1 = xf[..., :half]
    x2 = xf[..., half:ROPE_DIM]
    out = jnp.concatenate([x1 * cos - x2 * sin, x2 * cos + x1 * sin, xf[..., ROPE_DIM:]], axis=-1)
    return out.astype(x.dtype)

def moba_attention(q, k, v):
    bsz, s, h, d = q.shape
    nb = -(-s // MOBA_BLOCK)
    s_pad = nb * MOBA_BLOCK
    topk = min(MOBA_TOPK, nb)
    scale = 1.0 / math.sqrt(d)

    def to_heads(t):
        return jnp.pad(t, ((0, 0), (0, s_pad - s), (0, 0), (0, 0))).transpose(0, 2, 1, 3)

    qh, kh, vh = to_heads(q), to_heads(k), to_heads(v)
    qb = qh.reshape(bsz, h, nb, MOBA_BLOCK, d)
    kb = kh.reshape(bsz, h, nb, MOBA_BLOCK, d)
    vb = vh.reshape(bsz, h, nb, MOBA_BLOCK, d)

    s_own = jnp.einsum('bhnqd,bhnkd->bhnqk', qb, kb).astype(jnp.float32) * scale
    causal = jnp.tril(jnp.ones((MOBA_BLOCK, MOBA_BLOCK), dtype=bool))
    s_own = jnp.where(causal, s_own, NEG)
    lse_own = jax.nn.logsumexp(s_own, axis=-1)
    p_own = jnp.exp(s_own - lse_own[..., None]).astype(vb.dtype)
    o_own = jnp.einsum('bhnqk,bhnkd->bhnqd', p_own, vb).reshape(bsz, h, s_pad, d).astype(jnp.float32)
    lse_own = lse_own.reshape(bsz, h, s_pad)

    k_mean = jnp.mean(kb.astype(jnp.float32), axis=3)
    gate = jnp.einsum('bhsd,bhnd->bhsn', qh.astype(jnp.float32), k_mean)
    q_block = jnp.arange(s_pad, dtype=jnp.int32) // MOBA_BLOCK
    past = jnp.arange(nb, dtype=jnp.int32)[None, :] < q_block[:, None]
    gate = jnp.where(past, gate, NEG)
    _, sel = lax.top_k(gate, topk)
    valid = sel < q_block[:, None]
    flat_sel = sel + (jnp.arange(bsz * h, dtype=jnp.int32) * nb).reshape(bsz, h, 1, 1)
    k_flat = kb.reshape(bsz * h * nb, MOBA_BLOCK, d)
    v_flat = vb.reshape(bsz * h * nb, MOBA_BLOCK, d)
    n_chunks = bsz * h * s_pad // Q_CHUNK

    def attend_selected(args):
        qc, ic, vc = args
        kg = k_flat[ic]
        vg = v_flat[ic]
        sc = jnp.einsum('cd,cjkd->cjk', qc, kg).astype(jnp.float32) * scale
        sc = jnp.where(vc[:, :, None], sc, NEG).reshape(Q_CHUNK, topk * MOBA_BLOCK)
        lse = jax.nn.logsumexp(sc, axis=-1)
        p = jnp.exp(sc - lse[:, None]).reshape(Q_CHUNK, topk, MOBA_BLOCK).astype(vg.dtype)
        return jnp.einsum('cjk,cjkd->cd', p, vg).astype(jnp.float32), lse

    o_sel, lse_sel = lax.map(attend_selected, (qh.reshape(n_chunks, Q_CHUNK, d),
                                               flat_sel.reshape(n_chunks, Q_CHUNK, topk),
                                               valid.reshape(n_chunks, Q_CHUNK, topk)))
    o_sel = o_sel.reshape(bsz, h, s_pad, d)
    lse_sel = lse_sel.reshape(bsz, h, s_pad)
    lse = jnp.logaddexp(lse_own, lse_sel)
    o = jnp.exp(lse_own - lse)[..., None] * o_own + jnp.exp(lse_sel - lse)[..., None] * o_sel
    return o[:, :, :s].transpose(0, 2, 1, 3).reshape(bsz, s, h * d).astype(q.dtype)

def moe_ffn(xn, router_w, router_b, w_gu, b_gu, w_down, b_down):
    bsz, s, d = xn.shape
    n_tok = bsz * s
    xt = xn.reshape(n_tok, d)
    logits = (xt @ router_w).astype(jnp.float32) + router_b.astype(jnp.float32)
    top_val, top_idx = lax.top_k(logits, TOP_K)
    gates = jax.nn.softmax(top_val, axis=-1)

    n_assign = n_tok * TOP_K
    e_flat = top_idx.reshape(-1).astype(jnp.int32)
    tok_flat = jnp.arange(n_assign, dtype=jnp.int32) // TOP_K
    w_flat = gates.reshape(-1)
    order = jnp.argsort(e_flat)
    e_s, tok_s, w_s = e_flat[order], tok_flat[order], w_flat[order]
    counts = jnp.zeros((N_EXPERTS,), jnp.int32).at[e_flat].add(1)
    start = jnp.cumsum(counts) - counts
    padded = ((counts + EXPERT_ROWS - 1) // EXPERT_ROWS) * EXPERT_ROWS
    pend = jnp.cumsum(padded)
    pstart = pend - padded
    dest = pstart[e_s] + (jnp.arange(n_assign, dtype=jnp.int32) - start[e_s])
    n_rows = n_assign + N_EXPERTS * EXPERT_ROWS
    n_blk = n_rows // EXPERT_ROWS
    row_tok = jnp.full((n_rows,), n_tok, jnp.int32).at[dest].set(tok_s)
    row_w = jnp.zeros((n_rows,), jnp.float32).at[dest].set(w_s)
    blk_start = jnp.arange(n_blk, dtype=jnp.int32) * EXPERT_ROWS
    blk_expert = jnp.minimum(jnp.sum(blk_start[:, None] >= pend[None, :], axis=1), N_EXPERTS - 1)
    x_rows = jnp.concatenate([xt, jnp.zeros((1, d), xt.dtype)], axis=0)[row_tok]
    x_rows = x_rows.reshape(n_blk, EXPERT_ROWS, d)

    def expert_block(args):
        xb, e = args
        gu = xb @ w_gu[e] + b_gu[e]
        x_glu = jnp.minimum(gu[:, :D_EXPERT], SWIGLU_LIMIT)
        x_lin = jnp.clip(gu[:, D_EXPERT:], -SWIGLU_LIMIT, SWIGLU_LIMIT)
        act = x_glu * jax.nn.sigmoid(SWIGLU_ALPHA * x_glu) * (x_lin + 1.0)
        return act @ w_down[e] + b_down[e]

    y_blocks = lax.map(expert_block, (x_rows, blk_expert))
    y_rows = y_blocks.reshape(n_rows, d) * row_w[:, None].astype(y_blocks.dtype)
    y = jax.ops.segment_sum(y_rows, row_tok, num_segments=n_tok + 1)[:n_tok]
    return y.reshape(bsz, s, d)

def setup_inputs(seed: int = 0) -> dict:
    key = jax.random.key(seed)
    ks = jax.random.split(key, 21)
    f32 = jnp.float32

    def nrm(k, shape, scale):
        return jax.random.normal(k, shape, f32) * scale

    in_cols = 2 * RNN_WIDTH + 3 * ATTN_WIDTH + 2 * D_MODEL
    u = jax.random.uniform(ks[9], (DEPTH, RNN_WIDTH), f32, minval=0.9, maxval=0.999)
    s_lam = u ** (1.0 / LRU_C)
    return {
        'x': nrm(ks[0], (BATCH, SEQ, D_MODEL), 1.0),
        'norm_mix_g': 1.0 + nrm(ks[1], (DEPTH, D_MODEL), 0.02),
        'w_in': nrm(ks[2], (DEPTH, D_MODEL, in_cols), D_MODEL ** -0.5),
        'conv_w': nrm(ks[3], (DEPTH, CONV_WIDTH, RNN_WIDTH), CONV_WIDTH ** -0.5),
        'conv_b': nrm(ks[4], (DEPTH, RNN_WIDTH), 0.01),
        'lru_wx': nrm(ks[5], (DEPTH, RNN_BLOCKS, RNN_BLOCK_DIM, RNN_BLOCK_DIM), RNN_BLOCK_DIM ** -0.5),
        'lru_bx': nrm(ks[6], (DEPTH, RNN_WIDTH), 0.01),
        'lru_wa': nrm(ks[7], (DEPTH, RNN_BLOCKS, RNN_BLOCK_DIM, RNN_BLOCK_DIM), RNN_BLOCK_DIM ** -0.5),
        'lru_ba': nrm(ks[8], (DEPTH, RNN_WIDTH), 0.01),
        'lru_a_param': jnp.log(s_lam) - jnp.log1p(-s_lam),
        'w_proj_rnn': nrm(ks[10], (DEPTH, RNN_WIDTH, D_MODEL), RNN_WIDTH ** -0.5),
        'w_proj_attn': nrm(ks[11], (DEPTH, ATTN_WIDTH, D_MODEL), ATTN_WIDTH ** -0.5),
        'w_out': nrm(ks[12], (DEPTH, D_MODEL, D_MODEL), D_MODEL ** -0.5),
        'norm_ffn_g': 1.0 + nrm(ks[13], (DEPTH, D_MODEL), 0.02),
        'router_w': nrm(ks[14], (DEPTH, D_MODEL, N_EXPERTS), D_MODEL ** -0.5),
        'router_b': nrm(ks[15], (DEPTH, N_EXPERTS), 0.01),
        'expert_w_gu': nrm(ks[16], (DEPTH, N_EXPERTS, D_MODEL, 2 * D_EXPERT), D_MODEL ** -0.5),
        'expert_b_gu': nrm(ks[17], (DEPTH, N_EXPERTS, 2 * D_EXPERT), 0.01),
        'expert_w_down': nrm(ks[18], (DEPTH, N_EXPERTS, D_EXPERT, D_MODEL), D_EXPERT ** -0.5),
        'expert_b_down': nrm(ks[19], (DEPTH, N_EXPERTS, D_MODEL), 0.01),
        'norm_final_g': 1.0 + nrm(ks[20], (D_MODEL,), 0.02),
    }

def reference(x, norm_mix_g, w_in, conv_w, conv_b, lru_wx, lru_bx, lru_wa, lru_ba, lru_a_param,
              w_proj_rnn, w_proj_attn, w_out, norm_ffn_g, router_w, router_b,
              expert_w_gu, expert_b_gu, expert_w_down, expert_b_down, norm_final_g):
    bsz, s, _ = x.shape
    splits = [RNN_WIDTH, 2 * RNN_WIDTH, 2 * RNN_WIDTH + ATTN_WIDTH, 2 * RNN_WIDTH + 2 * ATTN_WIDTH,
              2 * RNN_WIDTH + 3 * ATTN_WIDTH, 2 * RNN_WIDTH + 3 * ATTN_WIDTH + D_MODEL]
    for layer in range(DEPTH):
        xn = rms_norm(x, norm_mix_g[layer])
        z = xn @ w_in[layer]
        rnn_x, rnn_gate, q, k, v, g_rnn, g_attn = jnp.split(z, splits, axis=-1)
        xc = causal_depthwise_conv(rnn_x, conv_w[layer], conv_b[layer])
        hr = rg_lru(xc, lru_wx[layer], lru_bx[layer], lru_wa[layer], lru_ba[layer], lru_a_param[layer])
        y_rnn = (hr * jax.nn.gelu(rnn_gate)) @ w_proj_rnn[layer]
        q = partial_rotary(q.reshape(bsz, s, N_HEADS, HEAD_DIM))
        k = partial_rotary(k.reshape(bsz, s, N_HEADS, HEAD_DIM))
        v = v.reshape(bsz, s, N_HEADS, HEAD_DIM)
        y_attn = moba_attention(q, k, v) @ w_proj_attn[layer]
        mixed = jax.nn.sigmoid(g_rnn) * y_rnn + jax.nn.sigmoid(g_attn) * y_attn
        x = x + mixed @ w_out[layer]
        hn = rms_norm(x, norm_ffn_g[layer])
        x = x + moe_ffn(hn, router_w[layer], router_b[layer], expert_w_gu[layer], expert_b_gu[layer],
                        expert_w_down[layer], expert_b_down[layer])
    return rms_norm(x, norm_final_g)


_drawn_inputs = setup_inputs


def setup_inputs(seed=0):
    import zlib

    import numpy as np

    out = dict(_drawn_inputs(seed))
    spreads = {}
    factors = {'lru_bx': 21.683,
     'lru_ba': 34.255,
     'expert_b_gu': 8.0,
     'expert_b_down': 8.0,
     'norm_final_g': 8.727,
     'router_b': 2.706}
    for name, (base, spread) in spreads.items():
        noise = np.random.default_rng([zlib.crc32(name.encode()), seed]).standard_normal(out[name].shape)
        drawn = base * np.exp(spread * noise) if base else spread * noise
        out[name] = __import__('jax').numpy.asarray(drawn.astype(out[name].dtype))
    for name, factor in factors.items():
        out[name] = (out[name] * factor).astype(out[name].dtype)
    return out
```

```python
from contextlib import ExitStack

import numpy as np
import concourse.bass as bass
from concourse import mybir

D = 1024
T = 256
P = 128
KT = D // P
TT = T // P
H = 8
N_E = 32
TOP_K = 4
SLOTS = 64
PASSES = T // SLOTS
PER_PASS = N_E + 1
HALF = D // 2
EPS = 1e-6
NEG = -1e30
ROPE = 32
LRU_C = 8.0
LIMIT = 7.0
ALPHA = 1.702
CONV = 4
W_RING = 4
LOW, HIGH = -3.0e38, 3.0e38

V_GMIX, V_CONVW, V_CONVB, V_BX, V_BA, V_AP, N_VEC = 0, 1, 5, 6, 7, 8, 9


def program(nc, x, vecs, rope, w_in, lru_wx, lru_wa, w_proj_rnn, w_proj_attn, w_out, norm_ffn_g,
            router_w, router_b, w_gu, b_gu, w_down, b_down, norm_final_g, out):
    f32, bf16, i32 = mybir.dt.float32, mybir.dt.bfloat16, mybir.dt.int32
    ALU, ACT, AX = mybir.AluOpType, mybir.ActivationFunctionType, mybir.AxisListType
    ds = bass.ds
    SCALE = float(P) ** -0.5

    ctx = ExitStack()
    with ctx:
        def sb(name, shape, dt=f32):
            return ctx.enter_context(nc.sbuf_tensor(name, shape, dt))

        def sem(name):
            return ctx.enter_context(nc.semaphore(name))

        ring = sb("ring", [P, 20 * 2048])
        wblk = [ring[:, i * 4096:(i + 1) * 4096].rearrange("p (k n) -> p k n", k=KT) for i in range(W_RING)]
        gu = [[ring[:, (par * 12 + k) * 2048:(par * 12 + k + 1) * 2048] for k in range(KT)] for par in range(2)]
        dn = [ring[:, (8 + j) * 2048:(9 + j) * 2048] for j in range(4)]

        def work(j):
            return ring[:, (8 + j) * 2048:(9 + j) * 2048].rearrange("p (k t) -> p k t", k=KT)

        xc, sx, sa, th = (work(j) for j in range(4))
        base = 12 * 2048
        zT = ring[:, base:base + 48 * T].rearrange("p (c t) -> p c t", t=T)
        Z_X, Z_GATE, Z_Q, Z_K, Z_GR, Z_GA = 0, 8, 16, 24, 32, 40
        oT, hg = zT[:, 0:8, :], zT[:, 8:16, :]
        xnT = ring[:, base + 48 * T:base + 56 * T].rearrange("p (k t) -> p k t", k=KT)
        v_sb = ring[:, base + 56 * T:base + 64 * T].rearrange("p (t n) -> p t n", t=TT)
        abase = base + 48 * T
        s_sb = [ring[:, abase + i * 384:abase + (i + 1) * 384] for i in range(2)]
        pT = [ring[:, abase + 768 + i * 384:abase + 768 + (i + 1) * 384] for i in range(2)]

        x_reg = sb("x_reg", [P, 2048])
        x_sb = x_reg[:, :].rearrange("p (t n) -> p t n", t=TT)
        gfin = x_reg[:, 0:1024]
        actT = x_reg[:, 1024:1536].rearrange("p (j s) -> p j s", j=4)
        y_sb = x_reg[:, 1536:2048]

        m_reg = sb("m_reg", [P, 4096])
        xs = m_reg[:, 0:2048].rearrange("p (t n) -> p t n", t=TT)
        rot = [m_reg[0:ROPE, i * 2048:(i + 1) * 2048].rearrange("p (h t) -> p h t", h=H) for i in range(2)]
        b96 = m_reg[0:96, 2048:4096]
        mixT = m_reg[:, 0:2048].rearrange("p (k t) -> p k t", k=KT)
        hnT = m_reg[:, 0:2048].rearrange("p (k t) -> p k t", k=KT)
        hn = m_reg[:, 2048:4096].rearrange("p (t n) -> p t n", t=TT)
        g1, l1, act_s = (m_reg[:, i * 512:(i + 1) * 512] for i in range(3))
        wT = m_reg[:, 1536:1792]
        gT = m_reg[0:N_E, 1792:2048]
        xg = m_reg[:, 2048:2560]
        sel_g = [m_reg[:, 2560 + i * 256:2816 + i * 256].rearrange("p (t s) -> p t s", t=TT) for i in range(2)]
        sel = [m_reg[:, 3072 + i * 64:3136 + i * 64].bitcast(bf16).rearrange("p (t s) -> p t s", t=TT)
               for i in range(2)]
        bsel = [m_reg[0:96, 3200 + i * 32:3232 + i * 32].bitcast(bf16) for i in range(2)]
        fin = m_reg[:, 0:2048].rearrange("p (t n) -> p t n", t=TT)

        p_reg = sb("p_reg", [P, 3072])
        part = [p_reg[:, i * 1024:(i + 1) * 1024].bitcast(bf16).rearrange("p (t n) -> p t n", t=TT)
                for i in range(3)]
        wx_bd = p_reg[:, 0:1024].rearrange("p (k n) -> p k n", k=KT)
        cos_t, sin_t = p_reg[0:ROPE, 1024:1280], p_reg[0:ROPE, 1280:1536]
        causal = p_reg[:, 1536:1664]
        gffn = p_reg[:, 2048:3072]

        o_reg = sb("o_reg", [P, 1024])
        wa_bd = o_reg[:, :].rearrange("p (k n) -> p k n", k=KT)
        bdn = o_reg[0:N_E, :]
        bias3 = sb("bias3", [96, 2048], bf16)

        vec_t = sb("vec_t", [P, N_VEC * KT])
        vec = vec_t[:, :].rearrange("p (n k) -> p n k", n=N_VEC)
        rw = sb("rw", [P, KT, N_E])
        rbb = sb("rbb", [P, N_E])
        ident = sb("ident", [P, P])
        tri = sb("tri", [P, P], bf16)
        ones = sb("ones", [P, P], bf16)
        zrow = sb("zrow", [1, P], bf16)
        iota = sb("iota", [P, SLOTS])
        ident3 = sb("ident3", [96, N_E + 1], bf16)
        stat = sb("stat", [P, 64])
        ss, rstd = stat[:, 0:2], stat[:, 2:4]
        ss2, rstd2 = stat[:, 4:6], stat[:, 6:8]
        ss3, rstd3 = stat[:, 8:10], stat[:, 10:12]
        negm, gsum, rsum = stat[:, 12:14], stat[:, 14:16], stat[:, 16:18]
        mx = stat[:, 18:22].rearrange("p (b t) -> p b t", b=2)
        sm = stat[:, 22:26].rearrange("p (b t) -> p b t", b=2)
        cmax = stat[0:1, 26:27]
        cneg, cpos = stat[:, 32:40], stat[:, 40:48]
        spu = stat[:, 48:56]
        sp2 = stat[:, 56:64]
        cnt_i = sb("cnt_i", [1, 1], i32)
        r0 = 3264
        lg = m_reg[:, r0:r0 + 72].rearrange("p (t e) -> p t e", t=TT)
        rep = m_reg[:, r0 + 72:r0 + 144].rearrange("p (t e) -> p t e", t=TT)
        mask = m_reg[:, r0 + 144:r0 + 208].rearrange("p (t e) -> p t e", t=TT)
        ex = m_reg[:, r0 + 208:r0 + 272].rearrange("p (t e) -> p t e", t=TT)
        gates = m_reg[:, r0 + 272:r0 + 338].rearrange("p (t e) -> p t e", t=TT)
        pos = m_reg[:, r0 + 338:r0 + 404].rearrange("p (t e) -> p t e", t=TT)
        m8 = m_reg[:, r0 + 404:r0 + 420].rearrange("p (t e) -> p t e", t=TT)
        v8 = m_reg[:, r0 + 420:r0 + 436].rearrange("p (t e) -> p t e", t=TT)
        maskb = m_reg[:, r0 + 436:r0 + 468].bitcast(bf16).rearrange("p (t e) -> p t e", t=TT)

        ps = ctx.enter_context(nc.psum_tensor("ps", [P, 8, 512], f32))

        x_landed = [sem(f"x_landed{t}") for t in range(TT)]
        w_landed = [sem(f"w_landed{i}") for i in range(W_RING)]
        gu_landed = [[sem(f"gu_landed{p}_{k}") for k in range(KT)] for p in range(2)]
        dn_landed = [sem(f"dn_landed{j}") for j in range(4)]
        (vec_landed, rope_landed, wx_landed, wa_landed, b96_landed, rw_landed, rbb_landed, gffn_landed,
         bdn_landed, gfin_landed, out_landed) = (sem(n + "_landed") for n in (
             "vec", "rope", "wx", "wa", "b96", "rw", "rbb", "gffn", "bdn", "gfin", "out"))
        rot_landed = [sem("rotq_landed"), sem("rotk_landed")]
        consts_ready, bd_zeroed, pool_step = sem("consts_ready"), sem("bd_zeroed"), sem("pool_step")
        bias_ready, dve_step, act_step = sem("bias_ready"), sem("dve_step"), sem("act_step")
        ss_ready, var_ready, sd_ready, xs_ready = (sem(n) for n in ("ss_ready", "var_ready", "sd_ready", "xs_ready"))
        xT_filled, xT_ready = sem("xT_filled"), sem("xT_ready")
        absap_ready, expap_ready, cc_ready = sem("absap_ready"), sem("expap_ready"), sem("cc_ready")
        z_filled, z_evicted = sem("z_filled"), sem("z_evicted")
        xc_ready, rope_done = sem("xc_ready"), sem("rope_done")
        gates_filled, gates_read, tanh_done, a_ready = (sem(n) for n in (
            "gates_filled", "gates_read", "tanh_done", "a_ready"))
        zsig_ready, m2_ready, mult_ready, gelu_ready, hg_ready = (sem(n) for n in (
            "zsig_ready", "m2_ready", "mult_ready", "gelu_ready", "hg_ready"))
        s_filled, negmax_ready, p_exp, p_ready = (sem(n) for n in (
            "s_filled", "negmax_ready", "p_exp", "p_ready"))
        pT_filled, pT_ready, o_filled, o_ready = (sem(n) for n in ("pT_filled", "pT_ready", "o_filled", "o_ready"))
        pr_filled, pa_filled, mixr_done, mix_ready = (sem(n) for n in ("pr_filled", "pa_filled", "mixr_done", "mix_ready"))
        wo_filled, x1_ready, ss2_ready, var2_ready, sd2_ready, hn_ready = (sem(n) for n in (
            "wo_filled", "x1_ready", "ss2_ready", "var2_ready", "sd2_ready", "hn_ready"))
        hnT_filled, hnT_act, hnT_dve = sem("hnT_filled"), sem("hnT_act"), sem("hnT_dve")
        hi_ready, rest_ready, mid_ready, parts_ready = (sem(n) for n in (
            "hi_ready", "rest_ready", "mid_ready", "parts_ready"))
        lg_filled, negm_ready, ex_ready, mask_ready, pos_filled, pos_ready = (sem(n) for n in (
            "lg_filled", "negm_ready", "ex_ready", "mask_ready", "pos_filled", "pos_ready"))
        gates_ready, count_ready, gT_filled, gT_ready, y_opened = (sem(n) for n in (
            "gates_ready", "count_ready", "gT_filled", "gT_ready", "y_opened"))
        sel_ready, gathered, xg_ready = sem("sel_ready"), sem("gathered"), sem("xg_ready")
        gu_used, dn_used, gu_read = sem("gu_used"), sem("dn_used"), sem("gu_read")
        wT_filled, wT_ready, glu_ready, sig_ready, t_ready, act_ready = (sem(n) for n in (
            "wT_filled", "wT_ready", "glu_ready", "sig_ready", "t_ready", "act_ready"))
        actT_filled, actT_ready, y_ready = sem("actT_filled"), sem("actT_ready"), sem("y_ready")
        moe_done, ss3_ready, var3_ready, sd3_ready, fin_ready = (sem(n) for n in (
            "moe_done", "ss3_ready", "var3_ready", "sd3_ready", "fin_ready"))

        w_gu_rows = w_gu.rearrange("l e k n -> (l e k) n")
        w_dn_rows = w_down.rearrange("l e k n -> (l e k) n")

        def overflow_passes(eng, body):
            eng.wait_ge(count_ready, 1)
            most = eng.value_load(cnt_i[0:1, 0:1], min_val=0, max_val=T)
            with eng.If(most > SLOTS):
                with eng.Fori(1, PASSES, 1) as p:
                    body(p)

        block = ctx.enter_context(nc.Block())

        @block.sync
        def _(sp):
            for t in range(TT):
                sp.dma_start(x_sb[:, t, :], x[0, t * P:(t + 1) * P, :]).then_inc(x_landed[t], 16)
            z_cols = [0, 512, 1024, 1536, 2048, 2560, 3072, 3584, 5120, 5632, 6144, 6656, 4096, 4608]
            blocks = [w_in[0, :, c:c + 512] for c in z_cols]
            for w in (w_proj_rnn, w_proj_attn, w_out):
                blocks += [w[0, :, 0:512], w[0, :, 512:1024]]
            for u, src in enumerate(blocks):
                if W_RING <= u < 18:
                    sp.wait_ge(z_filled, 2 * (u - W_RING) + 2)
                if u >= 18:
                    sp.wait_ge(pr_filled, 2 * (u - 17))
                sp.dma_start(wblk[u % W_RING], src.rearrange("(k p) n -> p k n", p=P)).then_inc(
                    w_landed[u % W_RING], 16)

            def load_gu(row, par, wait):
                for k in range(KT):
                    wait(k)
                    sp.dma_start(gu[par][k], w_gu_rows[ds(row + k * P, P), :]).then_inc(gu_landed[par][k], 16)

            def load_dn(row, wait):
                for j in range(4):
                    wait(j)
                    src = w_dn_rows[ds(row + j * 2 * P, 2 * P), :].rearrange("(k p) n -> p k n", p=P)
                    sp.dma_start(dn[j].rearrange("p (k n) -> p k n", k=2), src).then_inc(dn_landed[j], 16)

            def front_block_used(k):
                i = k // 2
                if i < 2:
                    sp.wait_ge(pa_filled, 2 * i + 2)
                else:
                    sp.wait_ge(wo_filled, 2 * i - 2)

            load_gu(0, 0, lambda k: front_block_used(k))
            load_dn(0, lambda j: sp.wait_ge(hg_ready, 1))
            load_gu(D, 1, lambda k: sp.wait_ge(mix_ready, 4))
            load_dn(D, lambda j: sp.wait_ge(dn_used, j + 1))

            def load_pair(E, row):
                load_gu(row, 0, lambda k: sp.wait_ge(gu_used, KT * E + (k + 1 - 2 * KT)))
                load_dn(row, lambda j: sp.wait_ge(dn_used, 4 * E + (j + 1 - 4)))
                load_gu(row + D, 1, lambda k: sp.wait_ge(gu_used, KT * E + (k + 1 - KT)))
                load_dn(row + D, lambda j: sp.wait_ge(dn_used, 4 * E + (j + 1)))

            with sp.Fori(1, N_E // 2, 1) as i:
                load_pair(2 * i, i * (2 * D))

            def again(p):
                with sp.Fori(0, N_E // 2, 1) as i:
                    load_pair(p * N_E + 2 * i, i * (2 * D))

            overflow_passes(sp, again)
            for t in range(TT):
                sp.wait_ge(fin_ready, t + 1)
                sp.dma_start(out[0, t * P:(t + 1) * P, :], fin[:, t, :]).then_inc(out_landed, 16)
            sp.wait_ge(out_landed, 16 * TT)

        @block.gpsimd
        def _(pool):
            steps = [0]

            def link(ins):
                steps[0] += 1
                ins.then_inc(pool_step, 1)
                pool.wait_ge(pool_step, steps[0])

            pool.dma_start(vec_t[:, :], vecs).then_inc(vec_landed, 16)
            pool.dma_start(b96[0:32, :], b_gu[0]).then_inc(b96_landed, 16)
            pool.dma_start(b96[32:64, :], b_gu[0]).then_inc(b96_landed, 16)
            pool.dma_start(b96[64:96, :], b_gu[0]).then_inc(b96_landed, 16)
            link(pool.memset(ident[:, :], 0.0))
            pool.affine_select(out=ident[:, :], in_=ident[:, :], compare_op=ALU.not_equal, fill=1.0, base=0,
                               pattern=[[-1, P]], channel_multiplier=1).then_inc(consts_ready, 1)
            link(pool.memset(wx_bd, 0.0))
            link(pool.memset(wa_bd, 0.0))
            for w, bd, landed in ((lru_wx, wx_bd, wx_landed), (lru_wa, wa_bd, wa_landed)):
                for odd in range(2):
                    src = w[0].rearrange("(j o) i k -> o i j k", o=2)[odd]
                    pool.dma_start(bd[64 * odd:64 * odd + 64, :, 64 * odd:64 * odd + 64], src).then_inc(landed, 16)
            pool.dma_start(cos_t, rope[0]).then_inc(rope_landed, 16)
            pool.dma_start(sin_t, rope[1]).then_inc(rope_landed, 16)
            pool.dma_start(rw[:, :, :], router_w[0].rearrange("(k p) e -> p k e", p=P)).then_inc(rw_landed, 16)
            pool.dma_start(rbb[:, :], router_b[0:1, :].to_broadcast([P, N_E])).then_inc(rbb_landed, 16)
            pool.dma_start(gffn, norm_ffn_g[0:1, :].to_broadcast([P, D])).then_inc(gffn_landed, 16)
            link(pool.memset(causal, 0.0))
            link(pool.affine_select(out=causal, in_=causal, compare_op=ALU.is_ge, fill=NEG, base=0,
                                    pattern=[[-1, P]], channel_multiplier=1))
            link(pool.memset(ones[:, :], 1.0))
            link(pool.affine_select(out=tri[:, :], in_=ones[:, :], compare_op=ALU.is_ge, fill=0.0, base=-1,
                                    pattern=[[1, P]], channel_multiplier=-1))
            link(pool.memset(zrow[:, :], 0.0))
            link(pool.iota(iota[:, :], pattern=[[1, SLOTS]], base=1, channel_multiplier=0,
                           allow_small_or_imprecise_dtypes=True))
            link(pool.memset(ident3[:, :], 0.0))
            for third in range(3):
                link(pool.affine_select(out=ident3[:, :], in_=ident3[:, :], compare_op=ALU.not_equal, fill=1.0,
                                        base=-32 * third, pattern=[[-1, N_E + 1]], channel_multiplier=1))
            pool.memset(stat[:, 26:32], 0.0).then_inc(consts_ready, 1)
            pool.wait_ge(b96_landed, 48)
            link(pool.tensor_copy(bias3[:, :], b96))
            for q in (1, 2):
                for r in range(q, 3):
                    rows = slice(32 * r, 32 * r + 32)
                    link(pool.tensor_tensor(b96[rows, :], b96[rows, :], bias3[rows, :], ALU.subtract))
                    link(pool.tensor_copy(bias3[rows, :], b96[rows, :]))
            pool.memset(zrow[:, :], 0.0).then_inc(bias_ready, 1)
            for i, z0 in enumerate((Z_Q, Z_K)):
                pool.wait_ge(z_evicted, 4 + (z0 + H) // 2)
                if i == 0:
                    pool.wait_ge(xT_filled, 4)
                for half in range(2):
                    src = zT[16 * (1 - half):16 * (1 - half) + 16, z0:z0 + H, :]
                    pool.dma_start(rot[i][16 * half:16 * half + 16, :, :], src).then_inc(rot_landed[i], 16)
            pool.wait_ge(gates_filled, KT)
            pool.dma_start(bdn, b_down[0]).then_inc(bdn_landed, 16)
            for t in range(TT):
                pool.wait_ge(hi_ready, t + 1)
                pool.wait_ge(hnT_filled, t + 1)
                pool.tensor_tensor(hn[:, t, :], hn[:, t, :], part[0][:, t, :], ALU.subtract).then_inc(rest_ready, 1)
            for t in range(TT):
                pool.wait_ge(mid_ready, t + 1)
                pool.tensor_tensor(part[2][:, t, :], hn[:, t, :], part[1][:, t, :], ALU.subtract).then_inc(
                    parts_ready, 1)
            pool.wait_ge(y_opened, 1)
            pool.dma_start(gfin, norm_final_g.rearrange("(o n) -> o n", o=1).to_broadcast([P, D])).then_inc(
                gfin_landed, 16)

        @block.tensor
        def _(pe):
            mm = nc.tensor.matmul
            pe.wait_ge(consts_ready, 1)
            for t in range(TT):
                pe.wait_ge(xs_ready, t + 1)
                for k in range(KT):
                    last = nc.tensor.transpose(ps[:, 4 + k // 2, (k % 2) * T + t * P:(k % 2) * T + (t + 1) * P],
                                               xs[:, t, k * P:(k + 1) * P], ident[:, :])
                    if t == TT - 1 and k % 2 == 1:
                        last.then_inc(xT_filled, 1)
            pe.wait_ge(xT_ready, KT)
            with pe.Fori(0, 3, 1) as it:
                for ul in range(4):
                    pe.wait_ge(w_landed[ul], 16 * it + 16)
                    for i in range(2):
                        pe.wait_ge(z_evicted, 8 * it + (2 * ul + i + 1))
                        for c in range(2):
                            for k in range(KT):
                                last = mm(ps[:, 2 * (ul % 2) + i, c * T:(c + 1) * T],
                                          wblk[ul][:, k, (2 * i + c) * P:(2 * i + c + 1) * P], xnT[:, k, :],
                                          start=k == 0, stop=k == KT - 1)
                        last.then_inc(z_filled, 1)
            pe.wait_ge(wx_landed, 32)
            pe.wait_ge(wa_landed, 32)
            for j in range(KT):
                pe.wait_ge(xc_ready, j + 1)
                if j >= 4:
                    pe.wait_ge(gates_read, j - 3)
                b = 4 + j % 4
                mm(ps[:, b, 0:T], wx_bd[:, j, :], xc[:, j, :], start=True, stop=True)
                mm(ps[:, b, T:2 * T], wa_bd[:, j, :], xc[:, j, :], start=True, stop=True).then_inc(gates_filled, 1)
            for ul in range(2):
                pe.wait_ge(w_landed[ul], 64)
                for t in range(TT):
                    pe.wait_ge(z_evicted, 24 + 2 * ul + t + 1)
                    for k in range(KT):
                        last = mm(ps[:, 2 * ul + t, :], xnT[:, k, t * P:(t + 1) * P], wblk[ul][:, k, :],
                                  start=k == 0, stop=k == KT - 1)
                    last.then_inc(z_filled, 1)

            def scores(i):
                if i == 0:
                    pe.wait_ge(rope_done, 2)
                    pe.wait_ge(gates_read, KT)
                if i >= 2:
                    pe.wait_ge(negmax_ready, i - 1)
                q, k = zT[:, Z_Q + i, :], zT[:, Z_K + i, :]
                mm(ps[:, 4 + i % 2, 0:P], q[:, 0:P], k[:, 0:P], start=True, stop=True)
                mm(ps[:, 4 + i % 2, P:384], q[:, P:T], k, start=True, stop=True).then_inc(s_filled, 1)

            def transpose_p(i):
                pe.wait_ge(p_ready, i + 1)
                if i >= 2:
                    pe.wait_ge(pT_ready, i - 1)
                for c in range(3):
                    last = nc.tensor.transpose(ps[:, 6 + i % 2, c * P:(c + 1) * P], s_sb[i % 2][:, c * P:(c + 1) * P],
                                               ident[:, :])
                last.then_inc(pT_filled, 1)

            def times_v(i):
                pe.wait_ge(pT_ready, i + 1)
                if i == 0:
                    pe.wait_ge(z_evicted, 32)
                if i >= 2:
                    pe.wait_ge(o_ready, i - 1)
                v0, v1 = (v_sb[:, t, i * P:(i + 1) * P] for t in range(TT))
                o = ps[:, i % 2, 0:T]
                mm(o[:, 0:P], v0, pT[i % 2][:, 0:P], start=True, stop=True)
                mm(o[:, P:T], v0, pT[i % 2][:, P:T], start=True, stop=False)
                mm(o[:, P:T], v1, pT[i % 2][:, T:384], start=False, stop=True).then_inc(o_filled, 1)

            scores(0)
            scores(1)
            for i in range(H + 1):
                if i < H:
                    transpose_p(i)
                if i + 2 < H:
                    scores(i + 2)
                if i >= 1:
                    times_v(i - 1)

            def project(src, b0, blocks, filled, free):
                for n, u in enumerate(blocks):
                    pe.wait_ge(w_landed[u % W_RING], 16 * (u // W_RING + 1))
                    for i in range(2):
                        free(2 * n + i)
                        for c in range(2):
                            for k in range(KT):
                                last = mm(ps[:, b0 + 2 * n + i, c * T:(c + 1) * T],
                                          wblk[u % W_RING][:, k, (2 * i + c) * P:(2 * i + c + 1) * P], src[:, k, :],
                                          start=k == 0, stop=k == KT - 1)
                        last.then_inc(filled, 1)

            pe.wait_ge(hg_ready, 1)
            project(hg, 4, (14, 15), pr_filled, lambda b: pe.wait_ge(negmax_ready, H) if b < 2 else pe.wait_ge(pT_ready, H))
            pe.wait_ge(o_ready, H)
            project(oT, 0, (16, 17), pa_filled, lambda b: None)
            for n, u in enumerate((18, 19)):
                pe.wait_ge(w_landed[u % W_RING], 16 * (u // W_RING + 1))
                pe.wait_ge(mixr_done, 4)
                for t in range(TT):
                    for k in range(KT):
                        if n == 0 and t == 0 and k % 2 == 0:
                            pe.wait_ge(mix_ready, k // 2 + 1)
                        last = mm(ps[:, 4 + 2 * n + t, :], mixT[:, k, t * P:(t + 1) * P], wblk[u % W_RING][:, k, :],
                                  start=k == 0, stop=k == KT - 1)
                    last.then_inc(wo_filled, 1)
            for t in range(TT):
                pe.wait_ge(hn_ready, t + 1)
                for k in range(KT):
                    last = nc.tensor.transpose(ps[:, k // 2, (k % 2) * T + t * P:(k % 2) * T + (t + 1) * P],
                                               hn[:, t, k * P:(k + 1) * P], ident[:, :])
                last.then_inc(hnT_filled, 1)
            pe.wait_ge(rw_landed, 16)
            pe.wait_ge(hnT_act, 2)
            pe.wait_ge(hnT_dve, 2)
            for t in range(TT):
                for k in range(KT):
                    last = mm(ps[:, 4, t * N_E:(t + 1) * N_E], hnT[:, k, t * P:(t + 1) * P], rw[:, k, :],
                              start=k == 0, stop=k == KT - 1)
            last.then_inc(lg_filled, 1)
            pe.wait_ge(mask_ready, 1)
            mm(ps[:, 5, 0:N_E], tri[:, :], maskb[:, 0, :], start=True, stop=True)
            mm(ps[:, 5, N_E:2 * N_E], ones[:, :], maskb[:, 0, :], start=True, stop=False)
            mm(ps[:, 5, N_E:2 * N_E], tri[:, :], maskb[:, 1, :], start=False, stop=True)
            mm(ps[:, 5, 64:96], ones[:, :], maskb[:, 0, :], start=True, stop=False)
            mm(ps[:, 5, 64:96], ones[:, :], maskb[:, 1, :], start=False, stop=True).then_inc(pos_filled, 1)

            def gather(buf):
                for k in range(KT):
                    for n, (t, q) in enumerate((t, q) for t in range(TT) for q in range(3)):
                        last = mm(ps[:, 6, k * SLOTS:(k + 1) * SLOTS], part[q][:, t, k * P:(k + 1) * P],
                                  sel[buf][:, t, :], start=n == 0, stop=n == 3 * TT - 1)
                last.then_inc(gathered, 1)

            for t in range(TT):
                for h in range(2):
                    mm(ps[:, 2 * t + h, :], ident[:, :], x_sb[:, t, h * HALF:(h + 1) * HALF], start=True, stop=False)
            pe.wait_ge(sel_ready, 1)
            pe.wait_ge(parts_ready, TT)
            gather(0)
            pe.wait_ge(gates_ready, 1)
            for t in range(TT):
                last = nc.tensor.transpose(ps[0:N_E, 7, t * P:(t + 1) * P], gates[:, t, 0:N_E], ident[:, :])
            last.then_inc(gT_filled, 1)
            pe.wait_ge(gT_ready, 1)
            pe.wait_ge(bdn_landed, 16)
            for t in range(TT):
                for h in range(2):
                    last = mm(ps[:, 2 * t + h, :], gT[:, t * P:(t + 1) * P], bdn[:, h * HALF:(h + 1) * HALF],
                              start=False, stop=False)
            last.then_inc(y_opened, 1)
            pe.wait_ge(bias_ready, 1)

            def expert(E, X, par):
                pe.wait_ge(xg_ready, X + (par + 1))
                pe.wait_ge(gu_read, E + (par + 1))
                for c in range(2):
                    for h in range(2):
                        mm(ps[64 * h:64 * h + 64, 4 + c, :], bsel[par],
                           bias3[:, c * D + h * HALF:c * D + (h + 1) * HALF], start=True, stop=False)
                for k in range(KT):
                    pe.wait_ge(gu_landed[par][k], 8 * E + 16)
                    for c in range(2):
                        for h in range(2):
                            last = mm(ps[64 * h:64 * h + 64, 4 + c, :], xg[:, k * SLOTS:(k + 1) * SLOTS],
                                      gu[par][k][:, c * D + h * HALF:c * D + (h + 1) * HALF],
                                      start=False, stop=k == KT - 1)
                    last.then_inc(gu_used, 1)
                for t in range(TT):
                    last = nc.tensor.transpose(ps[:, 7, t * P:(t + 1) * P], sel_g[par][:, t, :], ident[:, :])
                last.then_inc(wT_filled, 1)
                pe.wait_ge(sel_ready, X + (par + 2))
                gather(1 - par)
                pe.wait_ge(wT_ready, E + (par + 1))
                pe.wait_ge(act_ready, E + (par + 1))
                for j in range(4):
                    last = nc.tensor.transpose(ps[:, 7, j * P:(j + 1) * P], act_s[:, j * P:(j + 1) * P], ident[:, :])
                last.then_inc(actT_filled, 1)
                pe.wait_ge(actT_ready, E + (par + 1))
                pe.wait_ge(xg_ready, X + (par + 2))
                for k in range(KT):
                    if k % 2 == 0:
                        pe.wait_ge(dn_landed[k // 2], 16 * E + 16 * (par + 1))
                    for h in range(2):
                        c0 = (k % 2) * D + h * HALF
                        last = mm(ps[64 * h:64 * h + 64, 6, :], actT[:, k % 4, (k // 4) * SLOTS:(k // 4 + 1) * SLOTS],
                                  dn[k // 2][:, c0:c0 + HALF], start=k == 0, stop=k == KT - 1)
                    if k % 2 == 1:
                        last.then_inc(dn_used, 1)
                pe.wait_ge(y_ready, E + (par + 1))
                for t in range(TT):
                    for h in range(2):
                        mm(ps[:, 2 * t + h, :], wT[64 * h:64 * h + 64, t * P:(t + 1) * P], y_sb[64 * h:64 * h + 64, :],
                           start=False, stop=False)

            with pe.Fori(0, N_E // 2, 1) as i:
                for par in range(2):
                    expert(2 * i, 2 * i, par)

            def again(p):
                pe.wait_ge(sel_ready, PER_PASS * p + 1)
                gather(0)
                with pe.Fori(0, N_E // 2, 1) as i:
                    for par in range(2):
                        expert(p * N_E + 2 * i, p * PER_PASS + 2 * i, par)

            overflow_passes(pe, again)
            for b in range(4):
                last = mm(ps[:, b, :], zrow[0:1, :], bias3[0:1, 0:512], start=False, stop=True)
            last.then_inc(moe_done, 1)

        @block.scalar
        def _(act):
            A = nc.scalar.activation
            for t in range(TT):
                act.wait_ge(x_landed[t], 16)
                A(xc[:, 4 * t:4 * t + 4, :], x_sb[:, t, :].rearrange("p (c t) -> p c t", c=4), ACT.Square,
                  accum_out=ss[:, t:t + 1]).then_inc(ss_ready, 1)
            for t in range(TT):
                act.wait_ge(var_ready, t + 1)
                A(rstd[:, t:t + 1], rstd[:, t:t + 1], ACT.Sqrt).then_inc(sd_ready, 1)
            act.wait_ge(absap_ready, 1)
            A(spu, spu, ACT.Exp, scale=-1.0).then_inc(expap_ready, 1)
            for _ in range(4):
                act.nop().then_inc(z_evicted, 1)
            with act.Fori(0, 3, 1) as it:
                for b in range(8):
                    act.wait_ge(z_filled, 8 * it + (b + 1))
                    A(zT[:, ds(16 * it + 2 * b, 2), :], ps[:, b % 4, :].rearrange("p (c t) -> p c t", c=2),
                      ACT.Copy).then_inc(z_evicted, 1)
            act.wait_ge(vec_landed, 16)
            for j in range(KT):
                act.wait_ge(gates_filled, j + 1)
                A(sx[:, j, :], ps[:, 4 + j % 4, 0:T], ACT.Sigmoid, bias=vec[:, V_BX, j:j + 1])
                A(sa[:, j, :], ps[:, 4 + j % 4, T:2 * T], ACT.Sigmoid, bias=vec[:, V_BA, j:j + 1]).then_inc(
                    gates_read, 1)
            act.wait_ge(z_evicted, 28)
            A(zT[:, Z_GR:Z_GR + 16, :], zT[:, Z_GR:Z_GR + 16, :], ACT.Sigmoid).then_inc(zsig_ready, 1)
            act.wait_ge(cc_ready, 1)
            act.wait_ge(gates_read, KT)
            for j in range(KT):
                A(th[:, j, :], sa[:, j, :], ACT.Tanh, scale=cpos[:, j:j + 1]).then_inc(tanh_done, 1)
            act.wait_ge(tanh_done, KT)
            for j in range(KT):
                A(sa[:, j, :], sa[:, j, :], ACT.Exp, scale=cneg[:, j:j + 1]).then_inc(a_ready, 1)
            for k in range(4):
                act.wait_ge(z_filled, 24 + k + 1)
                A(v_sb[:, k % 2, (k // 2) * HALF:(k // 2 + 1) * HALF], ps[:, k, :], ACT.Copy).then_inc(z_evicted, 1)
            A(hg, hg, ACT.Gelu_apprx_tanh).then_inc(gelu_ready, 1)
            act.wait_ge(m2_ready, 1)
            A(th, th, ACT.Sqrt).then_inc(mult_ready, 1)
            for i in range(H + 1):
                if i < H:
                    act.wait_ge(negmax_ready, i + 1)
                    s = s_sb[i % 2]
                    A(s[:, 0:P], s[:, 0:P], ACT.Exp, bias=mx[:, i % 2, 0:1], scale=SCALE, accum_out=sm[:, i % 2, 0:1])
                    A(s[:, P:384], s[:, P:384], ACT.Exp, bias=mx[:, i % 2, 1:2], scale=SCALE,
                      accum_out=sm[:, i % 2, 1:2]).then_inc(p_exp, 1)
                if i >= 1:
                    act.wait_ge(pT_filled, i)
                    if i >= 3:
                        act.wait_ge(o_filled, i - 2)
                    A(pT[(i - 1) % 2], ps[:, 6 + (i - 1) % 2, 0:384], ACT.Copy).then_inc(pT_ready, 1)
            for t in range(TT):
                act.wait_ge(x1_ready, 3 + t)
                A(hn[:, t, :], x_sb[:, t, :], ACT.Square,
                  accum_out=ss2[:, t:t + 1]).then_inc(ss2_ready, 1)
            for t in range(TT):
                act.wait_ge(var2_ready, t + 1)
                A(rstd2[:, t:t + 1], rstd2[:, t:t + 1], ACT.Sqrt).then_inc(sd2_ready, 1)
            act.wait_ge(hnT_filled, TT)
            for j in range(2):
                A(hnT[:, 2 * j:2 * j + 2, :], ps[:, j, :].rearrange("p (c t) -> p c t", c=2), ACT.Copy).then_inc(
                    hnT_act, 1)
            for t in range(TT):
                A(part[0][:, t, :], hn[:, t, :], ACT.Copy).then_inc(hi_ready, 1)
            for t in range(TT):
                act.wait_ge(rest_ready, t + 1)
                A(part[1][:, t, :], hn[:, t, :], ACT.Copy).then_inc(mid_ready, 1)
            act.wait_ge(negm_ready, 1)
            for t in range(TT):
                A(ex[:, t, :], lg[:, t, 0:N_E], ACT.Exp, bias=negm[:, t:t + 1]).then_inc(ex_ready, 1)
            act.wait_ge(gathered, 1)
            A(xg, ps[:, 6, :], ACT.Copy).then_inc(xg_ready, 1)
            act.wait_ge(gT_filled, 1)
            A(gT, ps[0:N_E, 7, 0:T], ACT.Copy).then_inc(gT_ready, 1)
            act.wait_ge(y_opened, 1)

            def expert(E, X, par):
                act.wait_ge(wT_filled, E + (par + 1))
                A(wT, ps[:, 7, 0:T], ACT.Copy).then_inc(wT_ready, 1)
                act.wait_ge(glu_ready, E + (par + 1))
                A(act_s, g1, ACT.Sigmoid, scale=ALPHA).then_inc(sig_ready, 1)
                act.wait_ge(gathered, X + (par + 2))
                A(xg, ps[:, 6, :], ACT.Copy).then_inc(xg_ready, 1)
                act.wait_ge(dn_used, 4 * E + 4 * (par + 1))
                A(y_sb, ps[:, 6, :], ACT.Copy).then_inc(y_ready, 1)

            with act.Fori(0, N_E // 2, 1) as i:
                for par in range(2):
                    expert(2 * i, 2 * i, par)

            def again(p):
                act.wait_ge(gathered, PER_PASS * p + 1)
                A(xg, ps[:, 6, :], ACT.Copy).then_inc(xg_ready, 1)
                with act.Fori(0, N_E // 2, 1) as i:
                    for par in range(2):
                        expert(p * N_E + 2 * i, p * PER_PASS + 2 * i, par)

            overflow_passes(act, again)
            act.wait_ge(moe_done, 1)
            for t in range(TT):
                A(m_reg[:, 2048 + t * D:3072 + t * D].rearrange("p (h n) -> p h n", h=2), ps[:, 2 * t:2 * t + 2, :], ACT.Square,
                  accum_out=ss3[:, t:t + 1]).then_inc(ss3_ready, 1)
            for t in range(TT):
                act.wait_ge(var3_ready, t + 1)
                A(rstd3[:, t:t + 1], rstd3[:, t:t + 1], ACT.Sqrt).then_inc(sd3_ready, 1)

        @block.vector
        def _(dve):
            V = nc.vector
            steps = [0]

            def link(ins):
                steps[0] += 1
                ins.then_inc(dve_step, 1)
                dve.wait_ge(dve_step, steps[0])

            def rsqrt_mean(total, r, summed, var, sd):
                for t in range(TT):
                    dve.wait_ge(summed, t + 1)
                    V.tensor_scalar(r[:, t:t + 1], total[:, t:t + 1], 1.0 / D, EPS, ALU.mult, ALU.add).then_inc(var, 1)

            def reciprocal_of(r, t, sd):
                dve.wait_ge(sd, t + 1)
                link(V.reciprocal(r[:, t:t + 1], r[:, t:t + 1]))

            rsqrt_mean(ss, rstd, ss_ready, var_ready, sd_ready)
            for t in range(TT):
                reciprocal_of(rstd, t, sd_ready)
                V.tensor_scalar(xs[:, t, :], x_sb[:, t, :], rstd[:, t:t + 1], None, ALU.mult).then_inc(xs_ready, 1)
            dve.wait_ge(vec_landed, 16)
            ap = vec[:, V_AP, :]
            V.scalar_tensor_tensor(out=spu, in0=ap, scalar=-1.0, in1=ap, op0=ALU.mult, op1=ALU.max).then_inc(
                absap_ready, 1)
            for k in range(KT):
                if k % 2 == 0:
                    dve.wait_ge(xT_filled, k // 2 + 1)
                V.tensor_scalar(xnT[:, k, :], ps[:, 4 + k // 2, (k % 2) * T:(k % 2 + 1) * T], vec[:, V_GMIX, k:k + 1],
                                None, ALU.mult).then_inc(xT_ready, 1)
            dve.wait_ge(expap_ready, 1)
            link(V.tensor_scalar(cpos, spu, 2.0, None, ALU.add))
            link(V.reciprocal(cpos, cpos))
            link(V.tensor_tensor(spu, spu, cpos, ALU.mult))
            link(V.tensor_tensor(cpos, spu, spu, ALU.mult))
            link(V.tensor_scalar(sp2, cpos, 1.0 / 19, None, ALU.mult))
            for n in (17, 15, 13, 11, 9, 7, 5, 3):
                link(V.scalar_tensor_tensor(out=sp2, in0=sp2, scalar=1.0 / n, in1=cpos, op0=ALU.add, op1=ALU.mult))
            link(V.scalar_tensor_tensor(out=sp2, in0=sp2, scalar=1.0, in1=spu, op0=ALU.add, op1=ALU.mult))
            link(V.tensor_scalar(spu, ap, -1.0, 0.0, ALU.mult, ALU.max))
            link(V.scalar_tensor_tensor(out=sp2, in0=sp2, scalar=2.0, in1=spu, op0=ALU.mult, op1=ALU.add))
            V.tensor_scalar(cpos, sp2, LRU_C, None, ALU.mult)
            V.tensor_scalar(cneg, sp2, -LRU_C, None, ALU.mult).then_inc(cc_ready, 1)
            for j in range(KT):
                if j % 2 == 0:
                    dve.wait_ge(z_evicted, 4 + j // 2 + 1)
                    if j == 0:
                        dve.wait_ge(ss_ready, TT)
                z = zT[:, Z_X + j, :]
                link(V.tensor_scalar(xc[:, j, :], z, vec[:, V_CONVW + 3, j:j + 1], vec[:, V_CONVB, j:j + 1],
                                     ALU.mult, ALU.add))
                for back in (1, 2, 3):
                    ins = V.scalar_tensor_tensor(out=xc[:, j, back:T], in0=z[:, 0:T - back],
                                                 scalar=vec[:, V_CONVW + 3 - back, j:j + 1], in1=xc[:, j, back:T],
                                                 op0=ALU.mult, op1=ALU.add)
                    if back < 3:
                        link(ins)
                    else:
                        ins.then_inc(xc_ready, 1)
            dve.wait_ge(rope_landed, 32)

            def over_heads(table):
                return table.unsqueeze(1).to_broadcast([ROPE, H, T])

            for i, z0 in enumerate((Z_Q, Z_K)):
                dve.wait_ge(rot_landed[i], 32)
                z = zT[0:ROPE, z0:z0 + H, :]
                V.tensor_tensor(z, z, over_heads(cos_t), ALU.mult)
                link(V.tensor_tensor(rot[i], rot[i], over_heads(sin_t), ALU.mult))
                V.tensor_tensor(z, z, rot[i], ALU.add).then_inc(rope_done, 1)
            dve.wait_ge(gates_read, KT)
            link(V.tensor_tensor(sx, sx, xc, ALU.mult))
            dve.wait_ge(tanh_done, KT)
            link(V.tensor_scalar(xc, th, 1.0, None, ALU.add))
            link(V.reciprocal(xc, xc))
            V.scalar_tensor_tensor(out=th, in0=th, scalar=2.0, in1=xc, op0=ALU.mult, op1=ALU.mult).then_inc(m2_ready, 1)
            dve.wait_ge(mult_ready, 1)
            link(V.tensor_tensor(sx, sx, th, ALU.mult))
            dve.wait_ge(a_ready, KT)
            for j in range(KT):
                ins = V.tensor_tensor_scan(out=xc[:, j, :], data0=sa[:, j, :], data1=sx[:, j, :], initial=0.0,
                                           op0=ALU.mult, op1=ALU.add)
            link(ins)
            dve.wait_ge(gelu_ready, 1)
            V.tensor_tensor(hg, hg, xc, ALU.mult).then_inc(hg_ready, 1)

            def mask_and_max(i):
                dve.wait_ge(s_filled, i + 1)
                if i >= 2:
                    dve.wait_ge(pT_filled, i - 1)
                elif i == 0:
                    dve.wait_ge(z_filled, 28)
                b, s = ps[:, 4 + i % 2, :], s_sb[i % 2]
                diag = b[:, 0:512].rearrange("p (c n) -> p c n", c=2)[:, :, 0:P]
                sdiag = s.rearrange("p (c n) -> p c n", n=P)
                V.tensor_copy(s[:, P:T], b[:, P:T])
                V.tensor_tensor(s[:, 0:P], b[:, 0:P], causal, ALU.add)
                link(V.tensor_tensor(s[:, T:384], b[:, T:384], causal, ALU.add))
                V.reduce_max(mx[:, i % 2, 0:1], s[:, 0:P], AX.X)
                link(V.reduce_max(mx[:, i % 2, 1:2], s[:, P:384], AX.X))
                V.tensor_scalar(mx[:, i % 2, :], mx[:, i % 2, :], -SCALE, None, ALU.mult).then_inc(negmax_ready, 1)
                dve.wait_ge(negmax_ready, i + 1)

            def normalise(i):
                dve.wait_ge(p_exp, i + 1)
                link(V.reciprocal(sm[:, i % 2, :], sm[:, i % 2, :]))
                s = s_sb[i % 2]
                V.tensor_scalar(s[:, 0:P], s[:, 0:P], sm[:, i % 2, 0:1], None, ALU.mult)
                V.tensor_scalar(s[:, P:384], s[:, P:384], sm[:, i % 2, 1:2], None, ALU.mult).then_inc(p_ready, 1)

            def keep_o(i):
                dve.wait_ge(o_filled, i + 1)
                V.tensor_copy(oT[:, i, :], ps[:, i % 2, 0:T]).then_inc(o_ready, 1)

            dve.wait_ge(consts_ready, 2)
            for i in range(H + 2):
                if i < H:
                    mask_and_max(i)
                if 1 <= i <= H:
                    normalise(i - 1)
                if i >= 2:
                    keep_o(i - 2)

            dve.wait_ge(zsig_ready, 1)

            def two(t, k):
                return t[:, k:k + 2, :]

            for j in range(4):
                dve.wait_ge(pr_filled, j + 1)
                V.tensor_tensor(two(mixT, 2 * j), two(zT, Z_GR + 2 * j),
                                ps[:, 4 + j, :].rearrange("p (c t) -> p c t", c=2), ALU.mult).then_inc(mixr_done, 1)
            for j in range(4):
                dve.wait_ge(pa_filled, j + 1)
                link(V.tensor_tensor(two(zT, Z_GA + 2 * j), two(zT, Z_GA + 2 * j),
                                     ps[:, j, :].rearrange("p (c t) -> p c t", c=2), ALU.mult))
                V.tensor_tensor(two(mixT, 2 * j), two(mixT, 2 * j), two(zT, Z_GA + 2 * j), ALU.add).then_inc(
                    mix_ready, 1)
            for n in range(2):
                for t in range(TT):
                    dve.wait_ge(wo_filled, 2 * n + t + 1)
                    half = x_sb[:, t, n * HALF:(n + 1) * HALF]
                    V.tensor_tensor(half, half, ps[:, 4 + 2 * n + t, :], ALU.add).then_inc(x1_ready, 1)
            rsqrt_mean(ss2, rstd2, ss2_ready, var2_ready, sd2_ready)
            dve.wait_ge(gffn_landed, 16)
            for t in range(TT):
                reciprocal_of(rstd2, t, sd2_ready)
                V.scalar_tensor_tensor(out=hn[:, t, :], in0=x_sb[:, t, :], scalar=rstd2[:, t:t + 1], in1=gffn,
                                       op0=ALU.mult, op1=ALU.mult).then_inc(hn_ready, 1)
            dve.wait_ge(hnT_filled, TT)
            for j in range(2, 4):
                V.tensor_copy(two(hnT, 2 * j), ps[:, j, :].rearrange("p (c t) -> p c t", c=2)).then_inc(hnT_dve, 1)
            dve.wait_ge(parts_ready, TT)
            V.memset(lg[:, :, N_E:36], LOW)
            V.memset(v8[:, :, TOP_K:8], LOW)
            V.memset(gates, 0.0)
            V.memset(pos, 0.0)
            dve.wait_ge(lg_filled, 1)
            dve.wait_ge(rbb_landed, 16)
            for t in range(TT):
                ins = V.tensor_tensor(lg[:, t, 0:N_E], ps[:, 4, t * N_E:(t + 1) * N_E], rbb[:, :], ALU.add)
            link(ins)
            for t in range(TT):
                ins = V.max(m8[:, t, :], lg[:, t, 0:N_E])
            link(ins)
            V.tensor_scalar(negm, m8[:, :, 0], -1.0, None, ALU.mult).then_inc(negm_ready, 1)
            link(V.tensor_copy(v8[:, :, 0:TOP_K], m8[:, :, 0:TOP_K]))
            for t in range(TT):
                ins = V.match_replace(rep[:, t, :], v8[:, t, :], lg[:, t, :], HIGH)
            link(ins)
            V.tensor_scalar(maskb, rep[:, :, 0:N_E], HIGH, None, ALU.is_equal).then_inc(mask_ready, 1)
            link(V.tensor_scalar(mask, rep[:, :, 0:N_E], HIGH, None, ALU.is_equal))
            dve.wait_ge(pos_filled, 1)
            V.scalar_tensor_tensor(out=pos[:, :, 0:N_E], in0=ps[:, 5, 0:2 * N_E].rearrange("p (t e) -> p t e", t=TT),
                                   scalar=1.0, in1=mask, op0=ALU.add, op1=ALU.mult).then_inc(pos_ready, 1)
            link(V.reduce_max(cmax, ps[0:1, 5, 64:96], AX.X))
            V.tensor_copy(cnt_i[:, :], cmax).then_inc(count_ready, 1)
            dve.wait_ge(ex_ready, TT)
            link(V.tensor_tensor(ex, ex, mask, ALU.mult))
            for t in range(TT):
                ins = V.reduce_sum(gsum[:, t:t + 1], ex[:, t, :], AX.X)
            link(ins)
            link(V.reciprocal(rsum, gsum))
            for t in range(TT):
                ins = V.tensor_scalar(gates[:, t, 0:N_E], ex[:, t, :], rsum[:, t:t + 1], None, ALU.mult)
            ins.then_inc(gates_ready, 1)

            def build(e, buf):
                V.tensor_copy(bsel[buf], ident3[:, ds(e, 1)].to_broadcast([96, SLOTS]))
                for t in range(TT):
                    V.tensor_scalar(sel[buf][:, t, :], iota[:, :], pos[:, t, ds(e, 1)], None, ALU.is_equal)
                for t in range(TT):
                    ins = V.tensor_scalar(sel_g[buf][:, t, :].rearrange("p (d s) -> p d s", d=2),
                                          iota[:, :].unsqueeze(1).to_broadcast([P, 2, SLOTS]),
                                          pos[:, t, ds(e, 1)], gates[:, t, ds(e, 1)], ALU.is_equal, ALU.mult)
                ins.then_inc(sel_ready, 1)

            dve.wait_ge(gates_ready, 1)
            dve.wait_ge(pos_ready, 1)
            build(0, 0)
            V.tensor_copy(stat[:, 28:29], stat[:, 26:27]).then_inc(gu_read, 1)

            def expert(E, e, par):
                build(e + (par + 1), 1 - par)
                dve.wait_ge(gu_used, KT * E + KT * (par + 1))
                V.tensor_scalar(g1, ps[:, 4, :], LIMIT, None, ALU.min).then_inc(glu_ready, 1)
                V.tensor_scalar(l1, ps[:, 5, :], LIMIT, -LIMIT, ALU.min, ALU.max).then_inc(gu_read, 1)
                dve.wait_ge(gu_read, E + (par + 2))
                V.scalar_tensor_tensor(out=l1, in0=l1, scalar=1.0, in1=g1, op0=ALU.add, op1=ALU.mult).then_inc(
                    t_ready, 1)
                dve.wait_ge(t_ready, E + (par + 1))
                dve.wait_ge(sig_ready, E + (par + 1))
                V.tensor_tensor(act_s, l1, act_s, ALU.mult).then_inc(act_ready, 1)
                dve.wait_ge(actT_filled, E + (par + 1))
                V.tensor_copy(actT, ps[:, 7, :].rearrange("p (j s) -> p j s", j=4)).then_inc(actT_ready, 1)

            with dve.Fori(0, N_E // 2, 1) as i:
                for par in range(2):
                    expert(2 * i, 2 * i, par)

            def again(p):
                V.tensor_scalar(pos, pos, -float(SLOTS), None, ALU.add).then_inc(pos_ready, 1)
                dve.wait_ge(pos_ready, p + 1)
                build(0, 0)
                with dve.Fori(0, N_E // 2, 1) as i:
                    for par in range(2):
                        expert(p * N_E + 2 * i, 2 * i, par)

            overflow_passes(dve, again)
            rsqrt_mean(ss3, rstd3, ss3_ready, var3_ready, sd3_ready)
            dve.wait_ge(gfin_landed, 16)
            for t in range(TT):
                reciprocal_of(rstd3, t, sd3_ready)
                V.scalar_tensor_tensor(out=fin[:, t, :].rearrange("p (h n) -> p h n", h=2),
                                       in0=ps[:, 2 * t:2 * t + 2, :], scalar=rstd3[:, t:t + 1],
                                       in1=gfin.rearrange("p (h n) -> p h n", h=2),
                                       op0=ALU.mult, op1=ALU.mult).then_inc(fin_ready, 1)


def kernel(**inputs):
    import concourse.bacc as bacc
    from concourse.bass_utils import run_bass_kernel_spmd as run

    a = {k: np.ascontiguousarray(v) for k, v in inputs.items()}
    rows = [a["norm_mix_g"][0], *a["conv_w"][0], a["conv_b"][0], a["lru_bx"][0], a["lru_ba"][0], a["lru_a_param"][0]]
    vecs = np.ascontiguousarray(np.stack(rows).reshape(N_VEC, KT, P).transpose(2, 0, 1).reshape(P, N_VEC * KT))
    half = ROPE // 2
    inv = (500000.0 ** (-np.arange(half, dtype=np.float32) * np.float32(2.0 / ROPE))).astype(np.float32)
    ang = (np.arange(T, dtype=np.float32)[None, :] * inv[:, None]).astype(np.float64)
    cos, sin = np.cos(ang), np.sin(ang)
    rope = np.stack([np.concatenate([cos, cos]), np.concatenate([-sin, sin])]).astype(np.float32)

    nc = bacc.Bacc("TRN2", target_bir_lowering=False, num_devices=1)
    named = {
        "x": a["x"], "vecs": vecs, "rope": rope, "w_in": a["w_in"], "lru_wx": a["lru_wx"], "lru_wa": a["lru_wa"],
        "w_proj_rnn": a["w_proj_rnn"], "w_proj_attn": a["w_proj_attn"], "w_out": a["w_out"],
        "norm_ffn_g": a["norm_ffn_g"], "router_w": a["router_w"], "router_b": a["router_b"],
        "w_gu": a["expert_w_gu"], "b_gu": a["expert_b_gu"], "w_down": a["expert_w_down"],
        "b_down": a["expert_b_down"], "norm_final_g": a["norm_final_g"],
    }
    arrays, args = {}, {}
    for name, v in named.items():
        arrays[f"in_{name}"] = v
        args[name] = nc.dram_tensor(f"in_{name}", v.shape, mybir.dt.from_np(v.dtype), kind="ExternalInput").ap()
    out = nc.dram_tensor("out_y", (1, T, D), mybir.dt.float32, kind="ExternalOutput").ap()
    program(nc, out=out, **args)
    return run(nc, [arrays], core_ids=[0]).results[0]["out_y"]
```

```python
from contextlib import ExitStack

import numpy as np
import concourse.bass as bass
from concourse import mybir

D = 1024
T = 256
P = 128
KT = D // P
TT = T // P
H = 8
N_E = 32
TOP_K = 4
SLOTS = 64
PASSES = T // SLOTS
PER_PASS = N_E + 1
HALF = D // 2
EPS = 1e-6
NEG = -1e30
ROPE = 32
LRU_C = 8.0
LIMIT = 7.0
ALPHA = 1.702
CONV = 4
LAND = 2
N_BLK = 20
PIECES = 4
LOW, HIGH = -3.0e38, 3.0e38

V_GMIX, V_CONVW, V_CONVB, V_BX, V_BA, V_AP, N_VEC = 0, 1, 5, 6, 7, 8, 9


def program(nc, x, vecs, rope, w_in, lru_wx, lru_wa, w_proj_rnn, w_proj_attn, w_out, norm_ffn_g,
            router_w, router_b, w_gu, b_gu, w_down, b_down, norm_final_g, out):
    f32, f32r, bf16, i32 = mybir.dt.float32, mybir.dt.float32r, mybir.dt.bfloat16, mybir.dt.int32
    ALU, ACT, AX = mybir.AluOpType, mybir.ActivationFunctionType, mybir.AxisListType
    ds = bass.ds
    SCALE = float(P) ** -0.5

    ctx = ExitStack()
    with ctx:
        def sb(name, shape, dt=f32):
            return ctx.enter_context(nc.sbuf_tensor(name, shape, dt))

        def sem(name):
            return ctx.enter_context(nc.semaphore(name))

        KB = 1024
        slab0 = -(-nc.sbuf_base // 32) * 32
        sb("slab", [P, 204 * KB // 4])

        def at(name, kb, shape, dt=f32):
            return nc.alloc_sbuf_tensor_at(name, shape, dt, offset=slab0 + int(kb * KB))

        land = [at(f"land{i}", 16 * i, [P, KT, 512]) for i in range(LAND)]
        w_hi = at("w_hi", 32, [P, PIECES, KT, P], f32r)
        w_lo = at("w_lo", 48, [P, PIECES, KT, P], f32r)
        xc = at("xc", 64, [P, KT, T])
        sx = at("sx", 72, [P, KT, T])
        sa = at("sa", 80, [P, KT, T])
        th = at("th", 88, [P, KT, T])
        o_hi = at("o_hi", 64, [P, KT, T], f32r)
        hg_hi, hg_lo = at("hg_hi", 72, [P, KT, T], f32r), at("hg_lo", 80, [P, KT, T], f32r)
        s_sb = [at(f"s_sb{i}", 88 + 1.5 * i, [P, 384]) for i in range(2)]
        pT = [at(f"pT{i}", 91 + 1.5 * i, [P, 384]) for i in range(2)]
        z_q, z_k = at("z_q", 96, [P, KT, T]), at("z_k", 104, [P, KT, T])
        x_hi, x_lo = at("x_hi", 112, [P, KT, T], f32r), at("x_lo", 168, [P, KT, T], f32r)
        v_sb = at("v_sb", 120, [P, TT, D])
        z_x, z_gate = at("z_x", 128, [P, KT, T]), at("z_gate", 136, [P, KT, T])
        z_gr, z_ga = at("z_gr", 144, [P, KT, T]), at("z_ga", 152, [P, KT, T])
        o_lo = at("o_lo", 128, [P, KT, T], f32r)
        xs = at("xs", 168, [P, TT, D])
        b96 = at("b96", 176, [96, 2 * D])
        rot = [at("rot_q", 144, [ROPE, H, T]), at("rot_k", 152, [ROPE, H, T])]
        mix_hi, mix_lo = at("mix_hi", 168, [P, KT, T], f32r), at("mix_lo", 176, [P, KT, T], f32r)
        hnT, hn = at("hnT", 168, [P, KT, T]), at("hn", 176, [P, TT, D])
        wx_bd, wa_bd = at("wx_bd", 184, [P, KT, P]), at("wa_bd", 200, [P, KT, P])
        cos_t, sin_t = at("cos_t", 188, [ROPE, T]), at("sin_t", 189, [ROPE, T])
        causal = at("causal", 190, [P, P])
        gffn = at("gffn", 192, [P, D])
        x_sb = at("x_sb", 160, [P, TT, D])
        gu = [[at(f"gu{par}_{k}", 96 * par + 8 * k, [P, 2 * D]) for k in range(KT)] for par in range(2)]
        dn = [at(f"dn{j}", 64 + 8 * j, [P, 2, D]) for j in range(4)]
        gfin = at("gfin", 160, [P, D])
        actT = at("actT", 164, [P, 4, P])
        y_sb = at("y_sb", 166, [P, 512])
        g1, l1, act_s = (at(n, 168 + 2 * i, [P, 512]) for i, n in enumerate(("g1", "l1", "act_s")))
        wT = at("wT", 174, [P, T])
        xg = at("xg", 176, [P, 512])
        sel_g = [at(f"sel_g{i}", 178 + i, [P, TT, P]) for i in range(2)]
        sel = [at(f"sel{i}", 180 + i / 4, [P, TT, SLOTS], bf16) for i in range(2)]
        bsel = [at(f"bsel{i}", 180.5 + i / 8, [96, SLOTS], bf16) for i in range(2)]
        fin = at("fin", 168, [P, TT, D])
        squares = at("squares", 176, [P, TT, D])
        part = [at(f"part{i}", 184 + 4 * i, [P, TT, D], bf16) for i in range(3)]
        bias3 = at("bias3", 196, [96, 2 * D], bf16)
        bdn4, gT4 = at("bdn4", 200, [P, HALF]), at("gT4", 202, [P, T])
        lg, rep = at("lg", 181, [P, TT, 36]), at("rep", 181.5, [P, TT, 36])
        mask, ex = at("mask", 182, [P, TT, N_E]), at("ex", 182.25, [P, TT, N_E])
        m8, v8 = at("m8", 182.5, [P, TT, 8]), at("v8", 182.5625, [P, TT, 8])
        maskb = at("maskb", 182.625, [P, TT, N_E], bf16)
        gates4 = at("gates4", 182.75, [P, TT, 4, N_E])
        zrow = at("zrow", 183.75, [1, P], bf16)
        gates, pos = sb("gates", [P, TT, N_E + 1]), sb("pos", [P, TT, N_E + 1])

        vec = sb("vec", [P, N_VEC, KT])
        rw = sb("rw", [P, KT, N_E])
        rbb = sb("rbb", [P, N_E])
        ident = sb("ident", [P, P])
        tri = sb("tri", [P, P], bf16)
        ones = sb("ones", [P, P], bf16)
        iota = sb("iota", [P, SLOTS])
        ident3 = sb("ident3", [96, N_E + 1], bf16)
        stat = sb("stat", [P, 72])
        ss, rstd = stat[:, 0:2], stat[:, 2:4]
        ss2, rstd2 = stat[:, 4:6], stat[:, 6:8]
        ss3, rstd3 = stat[:, 8:10], stat[:, 10:12]
        negm, gsum, rsum = stat[:, 12:14], stat[:, 14:16], stat[:, 16:18]
        mx = stat[:, 18:22].rearrange("p (b t) -> p b t", b=2)
        sm = stat[:, 22:26].rearrange("p (b t) -> p b t", b=2)
        cmax = stat[0:1, 26:27]
        spare = stat[:, 27:30]
        cneg, cpos = stat[:, 32:40], stat[:, 40:48]
        spu = stat[:, 48:56]
        sp2 = stat[:, 56:64]
        ss2p = stat[:, 64:72].rearrange("p (t n) -> p t n", t=TT)
        cnt_i = sb("cnt_i", [1, 1], i32)

        ps = ctx.enter_context(nc.psum_tensor("ps", [P, 8, 512], f32))

        x_landed = [sem(f"x_landed{t}") for t in range(TT)]
        w_landed = [sem(f"w_landed{i}") for i in range(LAND)]
        hi_ready, lo_ready, filled, evicted = sem("hi_ready"), sem("lo_ready"), sem("filled"), sem("evicted")
        gu_landed = [[sem(f"gu_landed{p}_{k}") for k in range(KT)] for p in range(2)]
        dn_landed = [sem(f"dn_landed{j}") for j in range(4)]
        (vec_landed, rope_landed, wx_landed, wa_landed, b96_landed, rw_landed, rbb_landed, gffn_landed,
         bdn_landed, gfin_landed, out_landed) = (sem(n + "_landed") for n in (
             "vec", "rope", "wx", "wa", "b96", "rw", "rbb", "gffn", "bdn", "gfin", "out"))
        rot_landed = [sem("rotq_landed"), sem("rotk_landed")]
        consts_ready, bd_zeroed, pool_step = sem("consts_ready"), sem("bd_zeroed"), sem("pool_step")
        iota_ready, zrow_ready = sem("iota_ready"), sem("zrow_ready")
        bias_ready, dve_step = sem("bias_ready"), sem("dve_step")
        ss_ready, var_ready, sd_ready, xs_ready = (sem(n) for n in ("ss_ready", "var_ready", "sd_ready", "xs_ready"))
        xT_filled, xT_ready = sem("xT_filled"), sem("xT_ready")
        xT_hi = sem("xT_hi")
        absap_ready, expap_ready, cc_ready = sem("absap_ready"), sem("expap_ready"), sem("cc_ready")
        xc_ready, rope_done = sem("xc_ready"), sem("rope_done")
        gates_filled, gates_read, tanh_done, a_ready = (sem(n) for n in (
            "gates_filled", "gates_read", "tanh_done", "a_ready"))
        zsig_ready, sxc_ready, a2_ready, m2_ready, mult_ready, gelu_ready, hg_ready, hghi_ready, hglo_ready = (
            sem(n) for n in ("zsig_ready", "sxc_ready", "a2_ready", "m2_ready", "mult_ready", "gelu_ready",
                             "hg_ready", "hghi_ready", "hglo_ready"))
        s_filled, negmax_ready, p_exp, p_ready = (sem(n) for n in (
            "s_filled", "negmax_ready", "p_exp", "p_ready"))
        pT_filled, pT_ready, o_filled, ohi_ready, o_ready = (sem(n) for n in (
            "pT_filled", "pT_ready", "o_filled", "ohi_ready", "o_ready"))
        mixr_done, mixsum_ready, mixhi_ready, mix_ready = (sem(n) for n in (
            "mixr_done", "mixsum_ready", "mixhi_ready", "mix_ready"))
        x1_ready, ss2_ready, var2_ready, sd2_ready, hn_ready = (sem(n) for n in (
            "x1_ready", "ss2_ready", "var2_ready", "sd2_ready", "hn_ready"))
        hnT_filled, hnT_act, hnT_dve = sem("hnT_filled"), sem("hnT_act"), sem("hnT_dve")
        part0_ready, rest_ready, part1_ready, parts_ready = (sem(n) for n in (
            "part0_ready", "rest_ready", "part1_ready", "parts_ready"))
        lg_filled, negm_ready, ex_ready, mask_ready, pos_filled, pos_ready = (sem(n) for n in (
            "lg_filled", "negm_ready", "ex_ready", "mask_ready", "pos_filled", "pos_ready"))
        gates_ready, count_ready, gT_filled, gT_ready, y_opened = (sem(n) for n in (
            "gates_ready", "count_ready", "gT_filled", "gT_ready", "y_opened"))
        sel_ready, gathered, xg_ready = sem("sel_ready"), sem("gathered"), sem("xg_ready")
        gu_used, dn_used, gu_read = sem("gu_used"), sem("dn_used"), sem("gu_read")
        wT_filled, wT_ready, glu_ready, sig_ready, t_ready, act_ready = (sem(n) for n in (
            "wT_filled", "wT_ready", "glu_ready", "sig_ready", "t_ready", "act_ready"))
        actT_filled, actT_ready, y_ready = sem("actT_filled"), sem("actT_ready"), sem("y_ready")
        moe_done, ss3_ready, var3_ready, sd3_ready, fin_ready = (sem(n) for n in (
            "moe_done", "ss3_ready", "var3_ready", "sd3_ready", "fin_ready"))

        w_gu_rows = w_gu.rearrange("l e k n -> (l e k) n")
        w_dn_rows = w_down.rearrange("l e k n -> (l e k) n")

        def overflow_passes(eng, body):
            eng.wait_ge(count_ready, 1)
            most = eng.value_load(cnt_i[0:1, 0:1], min_val=0, max_val=T)
            with eng.If(most > SLOTS):
                with eng.Fori(1, PASSES, 1) as p:
                    body(p)

        block = ctx.enter_context(nc.Block())

        @block.sync
        def _(sp):
            for t in range(TT):
                sp.dma_start(x_sb[:, t, :], x[0, t * P:(t + 1) * P, :]).then_inc(x_landed[t], 16)
            sp.dma_start(vec[:, :, :], vecs.rearrange("p (n k) -> p n k", n=N_VEC)).then_inc(vec_landed, 16)
            blocks = [w_in[0, :, c:c + 512] for c in range(0, 7 * D, 512)]
            for w in (w_proj_rnn, w_proj_attn, w_out):
                blocks += [w[0, :, 0:512], w[0, :, 512:1024]]
            for u, src in enumerate(blocks):
                if u >= LAND:
                    sp.wait_ge(lo_ready, PIECES * (u - LAND + 1))
                sp.dma_start(land[u % LAND][:, :, :], src.rearrange("(k p) n -> p k n", p=P)).then_inc(
                    w_landed[u % LAND], 16)
                if u == 1:
                    for q in range(3):
                        sp.dma_start(b96[32 * q:32 * q + 32, :], b_gu[0]).then_inc(b96_landed, 16)
                    sp.wait_ge(bd_zeroed, 1)
                    for w, bd, landed in ((lru_wx, wx_bd, wx_landed), (lru_wa, wa_bd, wa_landed)):
                        for odd in range(2):
                            src = w[0].rearrange("(j o) i k -> o i j k", o=2)[odd]
                            sp.dma_start(bd[64 * odd:64 * odd + 64, :, 64 * odd:64 * odd + 64], src).then_inc(
                                landed, 16)
                    sp.dma_start(cos_t[:, :], rope[0]).then_inc(rope_landed, 16)
                    sp.dma_start(sin_t[:, :], rope[1]).then_inc(rope_landed, 16)
                    sp.dma_start(rw[:, :, :], router_w[0].rearrange("(k p) e -> p k e", p=P)).then_inc(rw_landed, 16)
                    sp.dma_start(rbb[:, :], router_b[0:1, :].to_broadcast([P, N_E])).then_inc(rbb_landed, 16)
                    sp.dma_start(gffn[:, :], norm_ffn_g[0:1, :].to_broadcast([P, D])).then_inc(gffn_landed, 16)
                for i, (z, after) in enumerate(((z_q, 8), (z_k, 10))):
                    if u == after:
                        sp.wait_ge(evicted, 4 + (12, 16)[i])
                        for half in range(2):
                            sp.dma_start(rot[i][16 * half:16 * half + 16, :, :],
                                         z[16 * (1 - half):16 * (1 - half) + 16, :, :]).then_inc(rot_landed[i], 16)
                if u == 12:
                    sp.wait_ge(gates_filled, KT)
                    for q in range(4):
                        sp.dma_start(bdn4[32 * q:32 * q + 32, :], b_down[0, :, (q % 2) * HALF:(q % 2 + 1) * HALF]
                                     ).then_inc(bdn_landed, 16)

            def load_gu(row, par, wait, ks=range(KT)):
                for k in ks:
                    wait(k)
                    sp.dma_start(gu[par][k][:, :], w_gu_rows[ds(row + k * P, P), :]).then_inc(gu_landed[par][k], 16)

            def load_dn(row, wait):
                for j in range(4):
                    wait(j)
                    src = w_dn_rows[ds(row + j * 2 * P, 2 * P), :].rearrange("(k p) n -> p k n", p=P)
                    sp.dma_start(dn[j][:, :, :], src).then_inc(dn_landed[j], 16)

            load_gu(D, 1, lambda k: sp.wait_ge(o_ready, H), range(0, 4))
            load_dn(0, lambda j: sp.wait_ge(filled, 36))
            load_gu(D, 1, lambda k: sp.wait_ge(mix_ready, 4), range(4, KT))
            load_gu(0, 0, lambda k: sp.wait_ge(lo_ready, 76 if k < 2 else 80), range(0, 4))
            load_gu(0, 0, lambda k: sp.wait_ge(filled, 40), range(4, KT))
            load_dn(D, lambda j: sp.wait_ge(dn_used, j + 1))

            def load_pair(E, row):
                load_gu(row, 0, lambda k: sp.wait_ge(gu_used, KT * E + (k + 1 - 2 * KT)))
                load_dn(row, lambda j: sp.wait_ge(dn_used, 4 * E + (j + 1 - 4)))
                load_gu(row + D, 1, lambda k: sp.wait_ge(gu_used, KT * E + (k + 1 - KT)))
                load_dn(row + D, lambda j: sp.wait_ge(dn_used, 4 * E + (j + 1)))

            with sp.Fori(1, N_E // 2, 1) as i:
                load_pair(2 * i, i * (2 * D))

            def again(p):
                with sp.Fori(0, N_E // 2, 1) as i:
                    load_pair(p * N_E + 2 * i, i * (2 * D))

            overflow_passes(sp, again)
            for t in range(TT):
                sp.wait_ge(fin_ready, t + 1)
                sp.dma_start(out[0, t * P:(t + 1) * P, :], fin[:, t, :]).then_inc(out_landed, 16)
            sp.wait_ge(out_landed, 16 * TT)

        @block.gpsimd
        def _(pool):
            steps = [0]

            def link(ins):
                steps[0] += 1
                ins.then_inc(pool_step, 1)
                pool.wait_ge(pool_step, steps[0])

            link(pool.memset(ident[:, :], 0.0))
            pool.affine_select(out=ident[:, :], in_=ident[:, :], compare_op=ALU.not_equal, fill=1.0, base=0,
                               pattern=[[-1, P]], channel_multiplier=1).then_inc(consts_ready, 1)
            pool.memset(wx_bd[:, :, :], 0.0)
            pool.memset(wa_bd[:, :, :], 0.0).then_inc(bd_zeroed, 1)
            link(pool.memset(causal[:, :], 0.0))
            link(pool.affine_select(out=causal[:, :], in_=causal[:, :], compare_op=ALU.is_ge, fill=NEG, base=0,
                                    pattern=[[-1, P]], channel_multiplier=1))
            link(pool.memset(ones[:, :], 1.0))
            link(pool.affine_select(out=tri[:, :], in_=ones[:, :], compare_op=ALU.is_ge, fill=0.0, base=-1,
                                    pattern=[[1, P]], channel_multiplier=-1))
            pool.memset(spare, 1.0).then_inc(consts_ready, 1)

            with pool.Fori(0, N_BLK // LAND, 1) as it:
                for q in range(PIECES * LAND):
                    pool.wait_ge(hi_ready, PIECES * LAND * it + (q + 1))
                    pool.tensor_tensor(w_lo[:, q % PIECES], land[q // PIECES][:, :, (q % PIECES) * P:(q % PIECES + 1) * P],
                                       w_hi[:, q % PIECES].bitcast(f32), ALU.subtract).then_inc(lo_ready, 1)
            link(pool.iota(iota[:, :], pattern=[[1, SLOTS]], base=1, channel_multiplier=0,
                           allow_small_or_imprecise_dtypes=True))
            link(pool.memset(ident3[:, :], 0.0))
            for third in range(3):
                ins = pool.affine_select(out=ident3[:, :], in_=ident3[:, :], compare_op=ALU.not_equal, fill=1.0,
                                         base=-32 * third, pattern=[[-1, N_E + 1]], channel_multiplier=1)
                if third < 2:
                    link(ins)
            ins.then_inc(iota_ready, 1)
            pool.wait_ge(parts_ready, TT)
            pool.memset(zrow[:, :], 0.0).then_inc(zrow_ready, 1)
            pool.wait_ge(y_opened, 1)
            pool.dma_start(gfin[:, :], norm_final_g.rearrange("(o n) -> o n", o=1).to_broadcast([P, D])).then_inc(
                gfin_landed, 16)

        @block.tensor
        def _(pe):
            mm = nc.tensor.matmul
            pe.wait_ge(consts_ready, 1)
            for t in range(TT):
                pe.wait_ge(xs_ready, t + 1)
                for k in range(KT):
                    last = nc.tensor.transpose(ps[:, 4 + k // 2, (k % 2) * T + t * P:(k % 2) * T + (t + 1) * P],
                                               xs[:, t, k * P:(k + 1) * P], ident[:, :])
                    if t == TT - 1 and k % 2 == 1:
                        last.then_inc(xT_filled, 1)
            pe.wait_ge(xT_ready, KT)

            def transposed(h, bank, src_hi, src_lo, base=0):
                for c in range(2):
                    b = (2 * h + c) % PIECES
                    pe.wait_ge(lo_ready, base + (2 * h + c + 1))
                    for k in range(KT):
                        for n, (w, s) in enumerate(((w_hi, src_hi), (w_hi, src_lo), (w_lo, src_hi))):
                            last = mm(ps[:, bank, c * T:(c + 1) * T], w[:, b, k, :], s[:, k, :],
                                      start=k == 0 and n == 0, stop=k == KT - 1 and n == 2)
                last.then_inc(filled, 1)

            def natural(h, bank, src_hi, src_lo, mixing=False):
                b = (2 * h) % PIECES
                pe.wait_ge(lo_ready, 2 * h + 2)
                for t in range(TT):
                    for k in range(KT):
                        if mixing and t == 0 and k % 2 == 0:
                            pe.wait_ge(mix_ready, k // 2 + 1)
                        for n, (s, w) in enumerate(((src_hi, w_hi), (src_hi, w_lo), (src_lo, w_hi))):
                            last = mm(ps[:, bank, t * T:(t + 1) * T].rearrange("p (c n) -> p c n", c=2),
                                      s[:, k, t * P:(t + 1) * P], w[:, b:b + 2, k, :],
                                      start=k == 0 and n == 0, stop=k == KT - 1 and n == 2)
                last.then_inc(filled, 1)

            def z_halves(first):
                with pe.Fori(0, 2, 1) as it:
                    for h in range(first, first + 4):
                        pe.wait_ge(evicted, 4 * it + (h + 1))
                        transposed(h, h % 4, x_hi, x_lo, base=8 * it)

            z_halves(0)
            pe.wait_ge(wx_landed, 32)
            pe.wait_ge(wa_landed, 32)
            for j in range(KT):
                pe.wait_ge(xc_ready, j + 1)
                if j >= 4:
                    pe.wait_ge(gates_read, j - 3)
                b = 4 + j % 4
                mm(ps[:, b, 0:T], wx_bd[:, j, :], xc[:, j, :], start=True, stop=True)
                mm(ps[:, b, T:2 * T], wa_bd[:, j, :], xc[:, j, :], start=True, stop=True).then_inc(gates_filled, 1)
            z_halves(8)
            for h in range(16, 20):
                pe.wait_ge(evicted, h + 1)
                natural(h, h % 4, x_hi, x_lo)

            def scores(i):
                if i == 0:
                    pe.wait_ge(rope_done, 2)
                    pe.wait_ge(gates_read, KT)
                if i >= 2:
                    pe.wait_ge(negmax_ready, i - 1)
                q, k = z_q[:, i, :], z_k[:, i, :]
                mm(ps[:, 4 + i % 2, 0:P], q[:, 0:P], k[:, 0:P], start=True, stop=True)
                mm(ps[:, 4 + i % 2, P:384], q[:, P:T], k, start=True, stop=True).then_inc(s_filled, 1)

            def transpose_p(i):
                pe.wait_ge(p_ready, i + 1)
                if i >= 1:
                    pe.wait_ge(pT_ready, i)
                for c in range(3):
                    last = nc.tensor.transpose(ps[:, 6, c * P:(c + 1) * P], s_sb[i % 2][:, c * P:(c + 1) * P],
                                               ident[:, :])
                last.then_inc(pT_filled, 1)

            def times_v(i):
                pe.wait_ge(pT_ready, i + 1)
                if i == 0:
                    pe.wait_ge(evicted, 4 + 20)
                if i >= 1:
                    pe.wait_ge(o_ready, i)
                v0, v1 = (v_sb[:, t, i * P:(i + 1) * P] for t in range(TT))
                o = ps[:, 7, 0:T]
                mm(o[:, 0:P], v0, pT[i % 2][:, 0:P], start=True, stop=True)
                mm(o[:, P:T], v0, pT[i % 2][:, P:T], start=True, stop=False)
                mm(o[:, P:T], v1, pT[i % 2][:, T:384], start=False, stop=True).then_inc(o_filled, 1)

            scores(0)
            scores(1)
            for i in range(H):
                h = 20 + i
                pe.wait_ge(evicted, h + 1)
                transposed(h, h % 4, x_hi, x_lo)
                transpose_p(i)
                if i + 2 < H:
                    scores(i + 2)
                if i >= 1:
                    times_v(i - 1)
            pe.wait_ge(hglo_ready, 1)
            for h in range(28, 32):
                pe.wait_ge(evicted, h + 1)
                transposed(h, h % 4, hg_hi, hg_lo)
                if h == 28:
                    times_v(H - 1)
            pe.wait_ge(o_ready, H)
            for h in range(32, 36):
                transposed(h, 4 + h % 4, o_hi, o_lo)
            for h in range(36, 40):
                pe.wait_ge(mixr_done, h - 35)
                natural(h, h % 4, mix_hi, mix_lo, mixing=h == 36)
            pe.wait_ge(x1_ready, 4)
            for t in range(TT):
                for h in range(2):
                    last = mm(ps[:, 2 * t + h, :], ident[:, :], x_sb[:, t, h * HALF:(h + 1) * HALF],
                              start=True, stop=False)
            last.then_inc(y_opened, 1)
            for t in range(TT):
                pe.wait_ge(hn_ready, t + 1)
                for k in range(KT):
                    last = nc.tensor.transpose(ps[:, 4 + k // 2, (k % 2) * T + t * P:(k % 2) * T + (t + 1) * P],
                                               hn[:, t, k * P:(k + 1) * P], ident[:, :])
                last.then_inc(hnT_filled, 1)
            pe.wait_ge(rw_landed, 16)
            pe.wait_ge(hnT_act, 2)
            pe.wait_ge(hnT_dve, 2)
            for t in range(TT):
                for k in range(KT):
                    last = mm(ps[:, 4, t * N_E:(t + 1) * N_E], hnT[:, k, t * P:(t + 1) * P], rw[:, k, :],
                              start=k == 0, stop=k == KT - 1)
            last.then_inc(lg_filled, 1)
            pe.wait_ge(mask_ready, 1)
            mm(ps[:, 5, 0:N_E], tri[:, :], maskb[:, 0, :], start=True, stop=True)
            mm(ps[:, 5, N_E:2 * N_E], ones[:, :], maskb[:, 0, :], start=True, stop=False)
            mm(ps[:, 5, N_E:2 * N_E], tri[:, :], maskb[:, 1, :], start=False, stop=True)
            mm(ps[:, 5, 64:96], ones[:, :], maskb[:, 0, :], start=True, stop=False)
            mm(ps[:, 5, 64:96], ones[:, :], maskb[:, 1, :], start=False, stop=True).then_inc(pos_filled, 1)

            def gather(buf):
                for k in range(KT):
                    for n, (t, q) in enumerate((t, q) for t in range(TT) for q in range(3)):
                        last = mm(ps[:, 6, k * SLOTS:(k + 1) * SLOTS], part[q][:, t, k * P:(k + 1) * P],
                                  sel[buf][:, t, :], start=n == 0, stop=n == 3 * TT - 1)
                last.then_inc(gathered, 1)

            pe.wait_ge(sel_ready, 1)
            pe.wait_ge(parts_ready, TT)
            gather(0)
            pe.wait_ge(gates_ready, 1)
            for t in range(TT):
                last = nc.tensor.transpose(ps[:, 7, t * P:(t + 1) * P], gates4[:, t], ident[:, :])
            last.then_inc(gT_filled, 1)
            pe.wait_ge(gT_ready, 1)
            pe.wait_ge(bdn_landed, 64)
            for q in range(4):
                t, rows = q // 2, slice(32 * q, 32 * q + 32)
                mm(ps[:, q, :], gT4[rows, t * P:(t + 1) * P], bdn4[rows, :], start=False, stop=False)
            pe.wait_ge(bias_ready, 1)

            def expert(E, X, par):
                pe.wait_ge(xg_ready, X + (par + 1))
                pe.wait_ge(gu_read, E + (par + 1))
                for c in range(2):
                    for h in range(2):
                        mm(ps[64 * h:64 * h + 64, 4 + c, :], bsel[par][:, :],
                           bias3[:, c * D + h * HALF:c * D + (h + 1) * HALF], start=True, stop=False)
                for k in range(KT):
                    pe.wait_ge(gu_landed[par][k], 8 * E + 16)
                    for c in range(2):
                        for h in range(2):
                            last = mm(ps[64 * h:64 * h + 64, 4 + c, :], xg[:, k * SLOTS:(k + 1) * SLOTS],
                                      gu[par][k][:, c * D + h * HALF:c * D + (h + 1) * HALF],
                                      start=False, stop=k == KT - 1)
                    last.then_inc(gu_used, 1)
                for t in range(TT):
                    last = nc.tensor.transpose(ps[:, 7, t * P:(t + 1) * P], sel_g[par][:, t, :], ident[:, :])
                last.then_inc(wT_filled, 1)
                pe.wait_ge(sel_ready, X + (par + 2))
                gather(1 - par)
                pe.wait_ge(wT_ready, E + (par + 1))
                pe.wait_ge(act_ready, E + (par + 1))
                for j in range(4):
                    last = nc.tensor.transpose(ps[:, 7, j * P:(j + 1) * P], act_s[:, j * P:(j + 1) * P], ident[:, :])
                last.then_inc(actT_filled, 1)
                pe.wait_ge(actT_ready, E + (par + 1))
                pe.wait_ge(xg_ready, X + (par + 2))
                for k in range(KT):
                    if k % 2 == 0:
                        pe.wait_ge(dn_landed[k // 2], 16 * E + 16 * (par + 1))
                    for h in range(2):
                        last = mm(ps[64 * h:64 * h + 64, 6, :], actT[:, k % 4, (k // 4) * SLOTS:(k // 4 + 1) * SLOTS],
                                  dn[k // 2][:, k % 2, h * HALF:(h + 1) * HALF], start=k == 0, stop=k == KT - 1)
                    if k % 2 == 1:
                        last.then_inc(dn_used, 1)
                pe.wait_ge(y_ready, E + (par + 1))
                for t in range(TT):
                    for h in range(2):
                        mm(ps[:, 2 * t + h, :], wT[64 * h:64 * h + 64, t * P:(t + 1) * P], y_sb[64 * h:64 * h + 64, :],
                           start=False, stop=False)

            with pe.Fori(0, N_E // 2, 1) as i:
                for par in range(2):
                    expert(2 * i, 2 * i, par)

            def again(p):
                pe.wait_ge(sel_ready, PER_PASS * p + 1)
                gather(0)
                with pe.Fori(0, N_E // 2, 1) as i:
                    for par in range(2):
                        expert(p * N_E + 2 * i, p * PER_PASS + 2 * i, par)

            overflow_passes(pe, again)
            pe.wait_ge(zrow_ready, 1)
            for b in range(4):
                last = mm(ps[:, b, :], zrow[0:1, :], bias3[0:1, 0:512], start=False, stop=True)
            last.then_inc(moe_done, 1)

        @block.scalar
        def _(act):
            A = nc.scalar.activation
            for t in range(TT):
                act.wait_ge(x_landed[t], 16)
                A(xc[:, 4 * t:4 * t + 4, :], x_sb[:, t, :].rearrange("p (c t) -> p c t", c=4), ACT.Square,
                  accum_out=ss[:, t:t + 1]).then_inc(ss_ready, 1)
            for t in range(TT):
                act.wait_ge(var_ready, t + 1)
                A(rstd[:, t:t + 1], rstd[:, t:t + 1], ACT.Sqrt).then_inc(sd_ready, 1)

            def split_hi(q):
                u = q // PIECES
                if q % PIECES == 0:
                    act.wait_ge(w_landed[u % LAND], 16 * (u // LAND + 1))
                if q >= PIECES:
                    act.wait_ge(filled, (q - PIECES) // 2 + 1)
                A(w_hi[:, q % PIECES], land[u % LAND][:, :, (q % PIECES) * P:(q % PIECES + 1) * P],
                  ACT.Copy).then_inc(hi_ready, 1)

            v_quarter = v_sb[:, :, :].rearrange("p t (c n) -> p c t n", c=4)

            def evict(h):
                act.wait_ge(filled, h + 1)
                bank = ps[:, h % 4, :].rearrange("p (c t) -> p c t", c=2)
                if 16 <= h < 20:
                    to = v_quarter[:, h - 16]
                else:
                    z = (z_x, z_gate, z_q, z_k, None, z_gr, z_ga)[h // 4]
                    to = z[:, 2 * (h % 4):2 * (h % 4) + 2, :]
                A(to, bank, ACT.Copy).then_inc(evicted, 1)

            def turn(h):
                if h < 28:
                    evict(h)
                if h + 2 < 2 * N_BLK:
                    split_hi(2 * h + 4)
                    split_hi(2 * h + 5)

            for q in range(PIECES):
                split_hi(q)
            act.wait_ge(vec_landed, 16)
            for k in range(KT):
                if k % 2 == 0:
                    act.wait_ge(xT_filled, k // 2 + 1)
                A(x_hi[:, k, :], ps[:, 4 + k // 2, (k % 2) * T:(k % 2 + 1) * T], ACT.Copy,
                  scale=vec[:, V_GMIX, k:k + 1]).then_inc(xT_hi, 1)
            act.wait_ge(absap_ready, 1)
            A(spu, spu, ACT.Exp, scale=-1.0).then_inc(expap_ready, 1)
            for _ in range(4):
                act.nop().then_inc(evicted, 1)
            for h in range(8):
                turn(h)
            for j in range(KT):
                act.wait_ge(gates_filled, j + 1)
                A(sx[:, j, :], ps[:, 4 + j % 4, 0:T], ACT.Sigmoid, bias=vec[:, V_BX, j:j + 1])
                A(sa[:, j, :], ps[:, 4 + j % 4, T:2 * T], ACT.Sigmoid, bias=vec[:, V_BA, j:j + 1]).then_inc(
                    gates_read, 1)
            act.wait_ge(cc_ready, 1)
            act.wait_ge(gates_read, KT)
            for h in range(8, 12):
                turn(h)
                for j in range(2 * (h - 8), 2 * (h - 8) + 2):
                    A(th[:, j, :], sa[:, j, :], ACT.Tanh, scale=cpos[:, j:j + 1]).then_inc(tanh_done, 1)
            act.wait_ge(tanh_done, KT)
            for h in range(12, 14):
                turn(h)
                for j in range(4 * (h - 12), 4 * (h - 12) + 4):
                    A(sa[:, j, :], sa[:, j, :], ACT.Exp, scale=cneg[:, j:j + 1]).then_inc(a_ready, 1)
            turn(14)
            act.wait_ge(sxc_ready, 1)
            act.wait_ge(a_ready, KT)
            A(xc[:, :, :], sa[:, :, :], ACT.Square).then_inc(a2_ready, 1)
            turn(15)
            act.wait_ge(evicted, 4 + 8)
            A(z_gate[:, :, :], z_gate[:, :, :], ACT.Gelu_apprx_tanh).then_inc(gelu_ready, 1)
            turn(16)
            act.wait_ge(m2_ready, 1)
            A(th[:, :, :], th[:, :, :], ACT.Sqrt).then_inc(mult_ready, 1)
            turn(17)
            turn(18)
            turn(19)
            act.wait_ge(hg_ready, 1)
            A(hg_hi[:, :, :], z_gate[:, :, :], ACT.Copy).then_inc(hghi_ready, 1)

            def exps(i):
                act.wait_ge(negmax_ready, i + 1)
                s = s_sb[i % 2]
                A(s[:, 0:P], s[:, 0:P], ACT.Exp, bias=mx[:, i % 2, 0:1], scale=SCALE, accum_out=sm[:, i % 2, 0:1])
                A(s[:, P:384], s[:, P:384], ACT.Exp, bias=mx[:, i % 2, 1:2], scale=SCALE,
                  accum_out=sm[:, i % 2, 1:2]).then_inc(p_exp, 1)

            def keep_pT(i):
                act.wait_ge(pT_filled, i + 1)
                if i >= 2:
                    act.wait_ge(o_filled, i - 1)
                A(pT[i % 2][:, :], ps[:, 6, 0:384], ACT.Copy).then_inc(pT_ready, 1)

            def keep_o(i):
                act.wait_ge(o_filled, i + 1)
                A(o_hi[:, i, :], ps[:, 7, 0:T], ACT.Copy).then_inc(ohi_ready, 1)

            exps(0)
            for i in range(1, H + 1):
                keep_pT(i - 1)
                turn(19 + i)
                if i >= 2:
                    keep_o(i - 2)
                if i < H:
                    exps(i)
            act.wait_ge(evicted, 4 + 28)
            A(z_gr[:, :, :], z_gr[:, :, :], ACT.Sigmoid).then_inc(zsig_ready, 1)
            turn(28)
            keep_o(H - 1)
            A(z_ga[:, :, :], z_ga[:, :, :], ACT.Sigmoid).then_inc(zsig_ready, 1)
            for h in range(29, 38):
                turn(h)
                if h >= 32 and h < 36:
                    j = h - 32
                    act.wait_ge(mixsum_ready, j + 1)
                    A(mix_hi[:, 2 * j:2 * j + 2, :], z_ga[:, 2 * j:2 * j + 2, :], ACT.Copy).then_inc(mixhi_ready, 1)
            A(spare[:, 0:1], spare[:, 0:1], ACT.Sqrt)
            for n in range(4):
                act.wait_ge(x1_ready, n + 1)
                for t in range(TT):
                    A(ps[:, 4 + n, t * T:(t + 1) * T], x_sb[:, t, n * T:(n + 1) * T], ACT.Square,
                      accum_out=ss2p[:, t, n:n + 1]).then_inc(ss2_ready, 1)
            act.wait_ge(var2_ready, 1)
            A(rstd2, rstd2, ACT.Sqrt).then_inc(sd2_ready, 1)
            A(spare[:, 1:2], spare[:, 1:2], ACT.Exp)
            for t in range(TT):
                act.wait_ge(hn_ready, t + 1)
                A(part[0][:, t, :], hn[:, t, :], ACT.Copy).then_inc(part0_ready, 1)
            act.wait_ge(hnT_filled, TT)
            for j in range(2):
                A(hnT[:, 2 * j:2 * j + 2, :], ps[:, 4 + j, :].rearrange("p (c t) -> p c t", c=2), ACT.Copy).then_inc(
                    hnT_act, 1)
            for t in range(TT):
                act.wait_ge(rest_ready, t + 1)
                A(part[1][:, t, :], hn[:, t, :], ACT.Copy).then_inc(part1_ready, 1)
            act.wait_ge(negm_ready, 1)
            for t in range(TT):
                A(ex[:, t, :], lg[:, t, 0:N_E], ACT.Exp, bias=negm[:, t:t + 1]).then_inc(ex_ready, 1)
            act.wait_ge(gathered, 1)
            A(xg[:, :], ps[:, 6, :], ACT.Copy).then_inc(xg_ready, 1)
            act.wait_ge(gT_filled, 1)
            A(gT4[:, :], ps[:, 7, 0:T], ACT.Copy).then_inc(gT_ready, 1)

            def expert(E, X, par):
                act.wait_ge(wT_filled, E + (par + 1))
                A(wT[:, :], ps[:, 7, 0:T], ACT.Copy).then_inc(wT_ready, 1)
                act.wait_ge(glu_ready, E + (par + 1))
                A(act_s[:, :], g1[:, :], ACT.Sigmoid, scale=ALPHA).then_inc(sig_ready, 1)
                act.wait_ge(gathered, X + (par + 2))
                A(xg[:, :], ps[:, 6, :], ACT.Copy).then_inc(xg_ready, 1)
                act.wait_ge(dn_used, 4 * E + 4 * (par + 1))
                A(y_sb[:, :], ps[:, 6, :], ACT.Copy).then_inc(y_ready, 1)

            with act.Fori(0, N_E // 2, 1) as i:
                for par in range(2):
                    expert(2 * i, 2 * i, par)

            def again(p):
                act.wait_ge(gathered, PER_PASS * p + 1)
                A(xg[:, :], ps[:, 6, :], ACT.Copy).then_inc(xg_ready, 1)
                with act.Fori(0, N_E // 2, 1) as i:
                    for par in range(2):
                        expert(p * N_E + 2 * i, p * PER_PASS + 2 * i, par)

            overflow_passes(act, again)
            A(spare[:, 2:3], spare[:, 2:3], ACT.Sqrt)
            act.wait_ge(moe_done, 1)
            for t in range(TT):
                A(squares[:, t, :].rearrange("p (h n) -> p h n", h=2), ps[:, 2 * t:2 * t + 2, :], ACT.Square,
                  accum_out=ss3[:, t:t + 1]).then_inc(ss3_ready, 1)
            for t in range(TT):
                act.wait_ge(var3_ready, t + 1)
                A(rstd3[:, t:t + 1], rstd3[:, t:t + 1], ACT.Sqrt).then_inc(sd3_ready, 1)

        @block.vector
        def _(dve):
            V = nc.vector
            steps = [0]

            def link(ins):
                steps[0] += 1
                ins.then_inc(dve_step, 1)
                dve.wait_ge(dve_step, steps[0])

            def rsqrt_mean(total, r, summed, var, sd):
                for t in range(TT):
                    dve.wait_ge(summed, t + 1)
                    V.tensor_scalar(r[:, t:t + 1], total[:, t:t + 1], 1.0 / D, EPS, ALU.mult, ALU.add).then_inc(var, 1)

            def reciprocal_of(r, t, sd):
                dve.wait_ge(sd, t + 1)
                link(V.reciprocal(r[:, t:t + 1], r[:, t:t + 1]))

            rsqrt_mean(ss, rstd, ss_ready, var_ready, sd_ready)
            for t in range(TT):
                reciprocal_of(rstd, t, sd_ready)
                V.tensor_scalar(xs[:, t, :], x_sb[:, t, :], rstd[:, t:t + 1], None, ALU.mult).then_inc(xs_ready, 1)
            dve.wait_ge(vec_landed, 16)
            ap = vec[:, V_AP, :]
            V.scalar_tensor_tensor(out=spu, in0=ap, scalar=-1.0, in1=ap, op0=ALU.mult, op1=ALU.max).then_inc(
                absap_ready, 1)
            for k in range(KT):
                if k % 2 == 0:
                    dve.wait_ge(xT_hi, k + 2)
                V.scalar_tensor_tensor(out=x_lo[:, k, :], in0=ps[:, 4 + k // 2, (k % 2) * T:(k % 2 + 1) * T],
                                       scalar=vec[:, V_GMIX, k:k + 1], in1=x_hi[:, k, :].bitcast(f32),
                                       op0=ALU.mult, op1=ALU.subtract).then_inc(xT_ready, 1)
            dve.wait_ge(expap_ready, 1)
            link(V.tensor_scalar(cpos, spu, 2.0, None, ALU.add))
            link(V.reciprocal(cpos, cpos))
            link(V.tensor_tensor(spu, spu, cpos, ALU.mult))
            link(V.tensor_tensor(cpos, spu, spu, ALU.mult))
            link(V.tensor_scalar(sp2, cpos, 1.0 / 19, None, ALU.mult))
            for n in (17, 15, 13, 11, 9, 7, 5, 3):
                link(V.scalar_tensor_tensor(out=sp2, in0=sp2, scalar=1.0 / n, in1=cpos, op0=ALU.add, op1=ALU.mult))
            link(V.scalar_tensor_tensor(out=sp2, in0=sp2, scalar=1.0, in1=spu, op0=ALU.add, op1=ALU.mult))
            link(V.tensor_scalar(spu, ap, -1.0, 0.0, ALU.mult, ALU.max))
            link(V.scalar_tensor_tensor(out=sp2, in0=sp2, scalar=2.0, in1=spu, op0=ALU.mult, op1=ALU.add))
            V.tensor_scalar(cpos, sp2, LRU_C, None, ALU.mult)
            V.tensor_scalar(cneg, sp2, -LRU_C, None, ALU.mult).then_inc(cc_ready, 1)
            dve.wait_ge(b96_landed, 48)
            link(V.tensor_copy(bias3[:, :], b96[:, :]))
            for q in (1, 2):
                for r in range(q, 3):
                    rows = slice(32 * r, 32 * r + 32)
                    link(V.tensor_tensor(b96[rows, :], b96[rows, :], bias3[rows, :], ALU.subtract))
                    link(V.tensor_copy(bias3[rows, :], b96[rows, :]))
            V.memset(gates[:, :, :], 0.0)
            V.memset(pos[:, :, :], 0.0).then_inc(bias_ready, 1)
            for j in range(KT):
                if j % 2 == 0:
                    dve.wait_ge(evicted, 4 + j // 2 + 1)
                    if j == 0:
                        dve.wait_ge(ss_ready, TT)
                z = z_x[:, j, :]
                link(V.tensor_scalar(xc[:, j, :], z, vec[:, V_CONVW + 3, j:j + 1], vec[:, V_CONVB, j:j + 1],
                                     ALU.mult, ALU.add))
                for back in (1, 2, 3):
                    ins = V.scalar_tensor_tensor(out=xc[:, j, back:T], in0=z[:, 0:T - back],
                                                 scalar=vec[:, V_CONVW + 3 - back, j:j + 1], in1=xc[:, j, back:T],
                                                 op0=ALU.mult, op1=ALU.add)
                    if back < 3:
                        link(ins)
                    else:
                        ins.then_inc(xc_ready, 1)
            dve.wait_ge(gates_read, KT)
            V.tensor_tensor(sx[:, :, :], sx[:, :, :], xc[:, :, :], ALU.mult).then_inc(sxc_ready, 1)

            def over_heads(table):
                return table[:, :].unsqueeze(1).to_broadcast([ROPE, H, T])

            def rotate(i, z):
                dve.wait_ge(rot_landed[i], 32)
                z = z[0:ROPE, :, :]
                V.tensor_tensor(z, z, over_heads(cos_t), ALU.mult)
                link(V.tensor_tensor(rot[i][:, :, :], rot[i][:, :, :], over_heads(sin_t), ALU.mult))
                V.tensor_tensor(z, z, rot[i][:, :, :], ALU.add).then_inc(rope_done, 1)

            dve.wait_ge(rope_landed, 32)
            rotate(0, z_q)
            dve.wait_ge(a2_ready, 1)
            V.scalar_tensor_tensor(out=th[:, :, :], in0=xc[:, :, :], scalar=1.0, in1=th[:, :, :],
                                   op0=ALU.add, op1=ALU.mult).then_inc(m2_ready, 1)
            dve.wait_ge(sxc_ready, 1)
            dve.wait_ge(mult_ready, 1)
            link(V.tensor_tensor(sx[:, :, :], sx[:, :, :], th[:, :, :], ALU.mult))
            for j in range(KT):
                ins = V.tensor_tensor_scan(out=xc[:, j, :], data0=sa[:, j, :], data1=sx[:, j, :], initial=0.0,
                                           op0=ALU.mult, op1=ALU.add)
            link(ins)
            dve.wait_ge(gelu_ready, 1)
            V.tensor_tensor(z_gate[:, :, :], z_gate[:, :, :], xc[:, :, :], ALU.mult).then_inc(hg_ready, 1)
            rotate(1, z_k)
            dve.wait_ge(hghi_ready, 1)
            V.tensor_tensor(hg_lo[:, :, :], z_gate[:, :, :], hg_hi[:, :, :].bitcast(f32), ALU.subtract).then_inc(
                hglo_ready, 1)

            def mask_and_max(i):
                dve.wait_ge(s_filled, i + 1)
                if i >= 2:
                    dve.wait_ge(pT_filled, i - 1)
                b, s = ps[:, 4 + i % 2, :], s_sb[i % 2]
                V.tensor_copy(s[:, P:T], b[:, P:T])
                V.tensor_tensor(s[:, 0:P], b[:, 0:P], causal[:, :], ALU.add)
                link(V.tensor_tensor(s[:, T:384], b[:, T:384], causal[:, :], ALU.add))
                V.reduce_max(mx[:, i % 2, 0:1], s[:, 0:P], AX.X)
                link(V.reduce_max(mx[:, i % 2, 1:2], s[:, P:384], AX.X))
                V.tensor_scalar(mx[:, i % 2, :], mx[:, i % 2, :], -SCALE, None, ALU.mult).then_inc(negmax_ready, 1)
                dve.wait_ge(negmax_ready, i + 1)

            def normalise(i):
                dve.wait_ge(p_exp, i + 1)
                link(V.reciprocal(sm[:, i % 2, :], sm[:, i % 2, :]))
                s = s_sb[i % 2]
                V.tensor_scalar(s[:, 0:P], s[:, 0:P], sm[:, i % 2, 0:1], None, ALU.mult)
                V.tensor_scalar(s[:, P:384], s[:, P:384], sm[:, i % 2, 1:2], None, ALU.mult).then_inc(p_ready, 1)

            def keep_o(i):
                dve.wait_ge(ohi_ready, i + 1)
                V.tensor_tensor(o_lo[:, i, :], ps[:, 7, 0:T], o_hi[:, i, :].bitcast(f32), ALU.subtract).then_inc(
                    o_ready, 1)

            dve.wait_ge(consts_ready, 2)
            for i in range(H):
                mask_and_max(i)
                if i >= 2:
                    keep_o(i - 2)
                normalise(i)
            keep_o(H - 2)
            keep_o(H - 1)

            def two(t, k):
                return t[:, k:k + 2, :]

            def bank(b):
                return ps[:, b, :].rearrange("p (c t) -> p c t", c=2)

            dve.wait_ge(zsig_ready, 1)
            for j in range(4):
                dve.wait_ge(filled, 28 + j + 1)
                V.tensor_tensor(two(z_gr, 2 * j), two(z_gr, 2 * j), bank(j), ALU.mult).then_inc(mixr_done, 1)
            dve.wait_ge(zsig_ready, 2)
            dve.wait_ge(mixr_done, 4)
            for j in range(4):
                z = two(z_ga, 2 * j)
                dve.wait_ge(filled, 32 + j + 1)
                link(V.tensor_tensor(z, z, bank(4 + j), ALU.mult))
                V.tensor_tensor(z, z, two(z_gr, 2 * j), ALU.add).then_inc(mixsum_ready, 1)
                dve.wait_ge(mixhi_ready, j + 1)
                V.tensor_tensor(two(mix_lo, 2 * j), z, two(mix_hi, 2 * j).bitcast(f32), ALU.subtract).then_inc(
                    mix_ready, 1)
            for n in range(4):
                dve.wait_ge(filled, 36 + n + 1)
                quarter = x_sb[:, :, n * T:(n + 1) * T]
                V.tensor_tensor(quarter, quarter, bank(n), ALU.add).then_inc(x1_ready, 1)
            dve.wait_ge(ss2_ready, 4 * TT)
            link(V.reduce_sum(ss2, ss2p, AX.X))
            V.tensor_scalar(rstd2, ss2, 1.0 / D, EPS, ALU.mult, ALU.add).then_inc(var2_ready, 1)
            dve.wait_ge(gffn_landed, 16)
            dve.wait_ge(sd2_ready, 1)
            link(V.reciprocal(rstd2, rstd2))
            for t in range(TT):
                V.scalar_tensor_tensor(out=hn[:, t, :], in0=x_sb[:, t, :], scalar=rstd2[:, t:t + 1], in1=gffn[:, :],
                                       op0=ALU.mult, op1=ALU.mult).then_inc(hn_ready, 1)
            for t in range(TT):
                dve.wait_ge(part0_ready, t + 1)
                dve.wait_ge(hnT_filled, t + 1)
                V.tensor_tensor(hn[:, t, :], hn[:, t, :], part[0][:, t, :], ALU.subtract).then_inc(rest_ready, 1)
            for j in range(2, 4):
                V.tensor_copy(two(hnT, 2 * j), bank(4 + j)).then_inc(hnT_dve, 1)
            for t in range(TT):
                dve.wait_ge(part1_ready, t + 1)
                V.tensor_tensor(part[2][:, t, :], hn[:, t, :], part[1][:, t, :], ALU.subtract).then_inc(parts_ready, 1)
            dve.wait_ge(parts_ready, TT)
            V.memset(lg[:, :, N_E:36], LOW)
            V.memset(v8[:, :, TOP_K:8], LOW)
            dve.wait_ge(lg_filled, 1)
            dve.wait_ge(rbb_landed, 16)
            for t in range(TT):
                ins = V.tensor_tensor(lg[:, t, 0:N_E], ps[:, 4, t * N_E:(t + 1) * N_E], rbb[:, :], ALU.add)
            link(ins)
            for t in range(TT):
                ins = V.max(m8[:, t, :], lg[:, t, 0:N_E])
            link(ins)
            V.tensor_scalar(negm, m8[:, :, 0], -1.0, None, ALU.mult).then_inc(negm_ready, 1)
            link(V.tensor_copy(v8[:, :, 0:TOP_K], m8[:, :, 0:TOP_K]))
            for t in range(TT):
                ins = V.match_replace(rep[:, t, :], v8[:, t, :], lg[:, t, :], HIGH)
            link(ins)
            V.tensor_scalar(maskb[:, :, :], rep[:, :, 0:N_E], HIGH, None, ALU.is_equal).then_inc(mask_ready, 1)
            link(V.tensor_scalar(mask[:, :, :], rep[:, :, 0:N_E], HIGH, None, ALU.is_equal))
            dve.wait_ge(pos_filled, 1)
            V.scalar_tensor_tensor(out=pos[:, :, 0:N_E], in0=ps[:, 5, 0:2 * N_E].rearrange("p (t e) -> p t e", t=TT),
                                   scalar=1.0, in1=mask[:, :, :], op0=ALU.add, op1=ALU.mult).then_inc(pos_ready, 1)
            link(V.reduce_max(cmax, ps[0:1, 5, 64:96], AX.X))
            V.tensor_copy(cnt_i[:, :], cmax).then_inc(count_ready, 1)
            dve.wait_ge(ex_ready, TT)
            link(V.tensor_tensor(ex[:, :, :], ex[:, :, :], mask[:, :, :], ALU.mult))
            for t in range(TT):
                ins = V.reduce_sum(gsum[:, t:t + 1], ex[:, t, :], AX.X)
            link(ins)
            link(V.reciprocal(rsum, gsum))
            for t in range(TT):
                V.tensor_scalar(gates[:, t, 0:N_E], ex[:, t, :], rsum[:, t:t + 1], None, ALU.mult)
                ins = V.tensor_scalar(gates4[:, t], ex[:, t, :].unsqueeze(1).to_broadcast([P, 4, N_E]),
                                      rsum[:, t:t + 1], None, ALU.mult)
            ins.then_inc(gates_ready, 1)

            def build(e, buf):
                V.tensor_copy(bsel[buf][:, :], ident3[:, ds(e, 1)].to_broadcast([96, SLOTS]))
                for t in range(TT):
                    V.tensor_scalar(sel[buf][:, t, :], iota[:, :], pos[:, t, ds(e, 1)], None, ALU.is_equal)
                for t in range(TT):
                    ins = V.tensor_scalar(sel_g[buf][:, t, :].rearrange("p (d s) -> p d s", d=2),
                                          iota[:, :].unsqueeze(1).to_broadcast([P, 2, SLOTS]),
                                          pos[:, t, ds(e, 1)], gates[:, t, ds(e, 1)], ALU.is_equal, ALU.mult)
                ins.then_inc(sel_ready, 1)

            dve.wait_ge(gates_ready, 1)
            dve.wait_ge(pos_ready, 1)
            dve.wait_ge(iota_ready, 1)
            build(0, 0)
            V.memset(stat[:, 30:31], 0.0).then_inc(gu_read, 1)

            def expert(E, e, par):
                build(e + (par + 1), 1 - par)
                dve.wait_ge(gu_used, KT * E + KT * (par + 1))
                V.tensor_scalar(g1[:, :], ps[:, 4, :], LIMIT, None, ALU.min).then_inc(glu_ready, 1)
                V.tensor_scalar(l1[:, :], ps[:, 5, :], LIMIT, -LIMIT, ALU.min, ALU.max).then_inc(gu_read, 1)
                dve.wait_ge(gu_read, E + (par + 2))
                V.scalar_tensor_tensor(out=l1[:, :], in0=l1[:, :], scalar=1.0, in1=g1[:, :], op0=ALU.add, op1=ALU.mult).then_inc(
                    t_ready, 1)
                dve.wait_ge(t_ready, E + (par + 1))
                dve.wait_ge(sig_ready, E + (par + 1))
                V.tensor_tensor(act_s[:, :], l1[:, :], act_s[:, :], ALU.mult).then_inc(act_ready, 1)
                dve.wait_ge(actT_filled, E + (par + 1))
                V.tensor_copy(actT[:, :, :], ps[:, 7, :].rearrange("p (j s) -> p j s", j=4)).then_inc(actT_ready, 1)

            with dve.Fori(0, N_E // 2, 1) as i:
                for par in range(2):
                    expert(2 * i, 2 * i, par)

            def again(p):
                V.tensor_scalar(pos[:, :, :], pos[:, :, :], -float(SLOTS), None, ALU.add).then_inc(pos_ready, 1)
                dve.wait_ge(pos_ready, p + 1)
                build(0, 0)
                with dve.Fori(0, N_E // 2, 1) as i:
                    for par in range(2):
                        expert(p * N_E + 2 * i, 2 * i, par)

            overflow_passes(dve, again)
            rsqrt_mean(ss3, rstd3, ss3_ready, var3_ready, sd3_ready)
            dve.wait_ge(gfin_landed, 16)
            for t in range(TT):
                reciprocal_of(rstd3, t, sd3_ready)
                V.scalar_tensor_tensor(out=fin[:, t, :].rearrange("p (h n) -> p h n", h=2),
                                       in0=ps[:, 2 * t:2 * t + 2, :], scalar=rstd3[:, t:t + 1],
                                       in1=gfin[:, :].rearrange("p (h n) -> p h n", h=2),
                                       op0=ALU.mult, op1=ALU.mult).then_inc(fin_ready, 1)


def kernel(**inputs):
    import concourse.bacc as bacc
    from concourse.bass_utils import run_bass_kernel_spmd as run

    a = {k: np.ascontiguousarray(v) for k, v in inputs.items()}
    rows = [a["norm_mix_g"][0], *a["conv_w"][0], a["conv_b"][0], a["lru_bx"][0], a["lru_ba"][0], a["lru_a_param"][0]]
    vecs = np.ascontiguousarray(np.stack(rows).reshape(N_VEC, KT, P).transpose(2, 0, 1).reshape(P, N_VEC * KT))
    half = ROPE // 2
    inv = (500000.0 ** (-np.arange(half, dtype=np.float32) * np.float32(2.0 / ROPE))).astype(np.float32)
    ang = (np.arange(T, dtype=np.float32)[None, :] * inv[:, None]).astype(np.float64)
    cos, sin = np.cos(ang), np.sin(ang)
    rope = np.stack([np.concatenate([cos, cos]), np.concatenate([-sin, sin])]).astype(np.float32)

    nc = bacc.Bacc("TRN2", target_bir_lowering=False, num_devices=1)
    named = {
        "x": a["x"], "vecs": vecs, "rope": rope, "w_in": a["w_in"], "lru_wx": a["lru_wx"], "lru_wa": a["lru_wa"],
        "w_proj_rnn": a["w_proj_rnn"], "w_proj_attn": a["w_proj_attn"], "w_out": a["w_out"],
        "norm_ffn_g": a["norm_ffn_g"], "router_w": a["router_w"], "router_b": a["router_b"],
        "w_gu": a["expert_w_gu"], "b_gu": a["expert_b_gu"], "w_down": a["expert_w_down"],
        "b_down": a["expert_b_down"], "norm_final_g": a["norm_final_g"],
    }
    arrays, args = {}, {}
    for name, v in named.items():
        arrays[f"in_{name}"] = v
        args[name] = nc.dram_tensor(f"in_{name}", v.shape, mybir.dt.from_np(v.dtype), kind="ExternalInput").ap()
    out = nc.dram_tensor("out_y", (1, T, D), mybir.dt.float32, kind="ExternalOutput").ap()
    program(nc, out=out, **args)
    return run(nc, [arrays], core_ids=[0]).results[0]["out_y"]
```

```python
from contextlib import ExitStack

import numpy as np
import concourse.bass as bass
from concourse import mybir

D = 1024
T = 256
P = 128
KT = D // P
TT = T // P
H = 8
N_E = 32
TOP_K = 4
SLOTS = 64
PASSES = T // SLOTS
PER_PASS = N_E + 1
HALF = D // 2
EPS = 1e-6
NEG = -1e30
ROPE = 32
LRU_C = 8.0
WARM = 36
LIMIT = 7.0
ALPHA = 1.702
CONV = 4
LAND = 2
N_BLK = 20
TURN = 8
PIECES = 4
LOW, HIGH = -3.0e38, 3.0e38

V_GMIX, V_CONVW, V_CONVB, V_BX, V_BA, V_AP, V_GFFN, N_VEC = 0, 1, 5, 6, 7, 8, 9, 10


def program(nc, x, vecs, rope, w_in, lru_wx, lru_wa, w_proj_rnn, w_proj_attn, w_out,
            router_w, router_b, w_gu, b_gu, w_down, b_down, norm_final_g, out):
    f32, f32r, bf16, i32 = mybir.dt.float32, mybir.dt.float32r, mybir.dt.bfloat16, mybir.dt.int32
    ALU, ACT, AX = mybir.AluOpType, mybir.ActivationFunctionType, mybir.AxisListType
    ds = bass.ds
    SCALE = float(P) ** -0.5

    ctx = ExitStack()
    with ctx:
        def sb(name, shape, dt=f32):
            return ctx.enter_context(nc.sbuf_tensor(name, shape, dt))

        def sem(name):
            return ctx.enter_context(nc.semaphore(name))

        KB = 1024
        slab0 = -(-nc.sbuf_base // 32) * 32
        sb("slab", [P, 204 * KB // 4])

        def at(name, kb, shape, dt=f32):
            return nc.alloc_sbuf_tensor_at(name, shape, dt, offset=slab0 + int(kb * KB))

        land = [at(f"land{i}", 16 * i, [P, KT, 512]) for i in range(LAND)]
        w_hi = at("w_hi", 32, [P, PIECES, KT, P], f32r)
        w_lo = at("w_lo", 48, [P, PIECES, KT, P], f32r)
        xc = at("xc", 64, [P, KT, T])
        sx = at("sx", 72, [P, KT, T])
        sa = at("sa", 80, [P, KT, T])
        th = at("th", 88, [P, KT, T])
        o_hi = at("o_hi", 64, [P, KT, T], f32r)
        hg_hi, hg_lo = at("hg_hi", 72, [P, KT, T], f32r), at("hg_lo", 176, [P, KT, T], f32r)
        s_sb = [at(f"s_sb{i}", 188 + 1.5 * i, [P, 384]) for i in range(2)]
        pT = [at(f"pT{i}", 200 + 1.5 * i, [P, 384]) for i in range(2)]
        z_q, z_k = at("z_q", 96, [P, KT, T]), at("z_k", 104, [P, KT, T])
        x_hi, x_lo = at("x_hi", 112, [P, KT, T], f32r), at("x_lo", 168, [P, KT, T], f32r)
        v_sb = at("v_sb", 184, [P, 4 * D])[:, :].rearrange("p (t c) -> p t c", t=TT)[:, :, 0:D]
        z_x, z_gate = at("z_x", 128, [P, KT, T]), at("z_gate", 136, [P, KT, T])
        z_gr, z_ga = at("z_gr", 144, [P, KT, T]), at("z_ga", 152, [P, KT, T])
        o_lo = at("o_lo", 128, [P, KT, T], f32r)
        xs = at("xs", 168, [P, TT, D])
        b96 = at("b96", 176, [96, 2 * D])
        rot = [at("rot_q", 144, [ROPE, H, T]), at("rot_k", 152, [ROPE, H, T])]
        mix_hi, mix_lo = at("mix_hi", 168, [P, KT, T], f32r), at("mix_lo", 176, [P, KT, T], f32r)
        x1T, hn = at("x1T", 24, [P, KT, T]), at("hn", 168, [P, TT, D])
        wx_bd, wa_bd = at("wx_bd", 184, [P, KT, P]), at("wa_bd", 200, [P, KT, P])
        cos_t, sin_t = at("cos_t", 188, [ROPE, T]), at("sin_t", 189, [ROPE, T])
        causal = at("causal", 191, [P, P])
        sq_out = at("sq_out", 192, [P, 4, TT, T], bf16)
        x_sb = at("x_sb", 160, [P, TT, D])
        gu = [[at(f"gu{par}_{k}", 96 * par + 8 * k, [P, 2 * D]) for k in range(KT)] for par in range(2)]
        dn = [at(f"dn{j}", 64 + 8 * j, [P, 2, D]) for j in range(4)]
        gfin = at("gfin", 160, [P, D])
        actT = at("actT", 164, [P, 4, P])
        y_sb = at("y_sb", 166, [P, 512])
        g1, l1, act_s = (at(n, 168 + 2 * i, [P, 512]) for i, n in enumerate(("g1", "l1", "act_s")))
        wT = at("wT", 174, [P, T])
        xg = at("xg", 176, [P, 512])
        sel_g = [at(f"sel_g{i}", 178 + i, [P, TT, P]) for i in range(2)]
        sel = [at(f"sel{i}", 180 + i / 4, [P, TT, SLOTS], bf16) for i in range(2)]
        bsel = [at(f"bsel{i}", 180.5 + i / 8, [96, SLOTS], bf16) for i in range(2)]
        fin = at("fin", 168, [P, TT, D])
        squares = at("squares", 176, [P, TT, D])
        part = [at(f"part{i}", 184 + 4 * i, [P, TT, D], bf16) for i in range(3)]
        bias3 = at("bias3", 196, [96, 2 * D], bf16)
        bdn4, gT4 = at("bdn4", 200, [P, HALF]), at("gT4", 202, [P, T])
        sel0 = at("sel0", 203.25, [P, TT, SLOTS])
        lg, rep = at("lg", 181, [P, TT, 36]), at("rep", 181.5, [P, TT, 36])
        mask, ex = at("mask", 182, [P, TT, N_E]), at("ex", 182.25, [P, TT, N_E])
        m8, v8 = at("m8", 182.5, [P, TT, 8]), at("v8", 182.5625, [P, TT, 8])
        maskb = at("maskb", 182.625, [P, TT, N_E], bf16)
        gates4 = at("gates4", 182.75, [P, TT, 4, N_E])
        zrow = at("zrow", 203, [1, P], bf16)
        gates, pos = sb("gates", [P, TT, N_E + 1]), sb("pos", [P, TT, N_E + 1])

        vec = sb("vec", [P, N_VEC, KT])
        rw = sb("rw", [P, KT, N_E])
        rbb = sb("rbb", [P, N_E])
        ident = sb("ident", [P, P])
        tri = sb("tri", [P, P], bf16)
        ones = sb("ones", [P, P], bf16)
        iota = sb("iota", [P, SLOTS])
        ident3 = sb("ident3", [96, N_E + 1], bf16)
        stat = sb("stat", [P, 72])
        ss, rstd = stat[:, 0:2], stat[:, 2:4]
        ss2, rstd2 = stat[:, 4:6], stat[:, 6:8]
        ss3, rstd3 = stat[:, 8:10], stat[:, 10:12]
        negm, gsum, rsum = stat[:, 12:14], stat[:, 14:16], stat[:, 16:18]
        mx = stat[:, 18:22].rearrange("p (b t) -> p b t", b=2)
        sm = stat[:, 22:26].rearrange("p (b t) -> p b t", b=2)
        cmax = stat[0:1, 26:27]
        spare = stat[:, 27:28]
        cneg, cpos = stat[:, 32:40], stat[:, 40:48]
        spu = stat[:, 48:56]
        sp2 = stat[:, 56:64]
        ss2p = stat[:, 64:72].rearrange("p (t n) -> p t n", t=TT)
        cnt_i = sb("cnt_i", [1, 1], i32)

        ps = ctx.enter_context(nc.psum_tensor("ps", [P, 8, 512], f32))

        x_landed = [sem(f"x_landed{t}") for t in range(TT)]
        gathered_half, xg_half = sem("gathered_half"), sem("xg_half")
        first_landed, spare_ready = sem("first_landed"), sem("spare_ready")
        w_landed = [sem(f"w_landed{i}") for i in range(LAND)]
        hi_ready, lo_ready, filled, evicted = sem("hi_ready"), sem("lo_ready"), sem("filled"), sem("evicted")
        gu_landed = [[sem(f"gu_landed{p}_{k}") for k in range(KT)] for p in range(2)]
        dn_landed = [sem(f"dn_landed{j}") for j in range(5)]
        (vec_landed, rope_landed, wx_landed, wa_landed, b96_landed, rw_landed, rbb_landed,
         bdn_landed, gfin_landed, out_landed) = (sem(n + "_landed") for n in (
             "vec", "rope", "wx", "wa", "b96", "rw", "rbb", "bdn", "gfin", "out"))
        rot_landed = [sem("rotq_landed"), sem("rotk_landed")]
        consts_ready, bd_zeroed, pool_step = sem("consts_ready"), sem("bd_zeroed"), sem("pool_step")
        iota_ready, zrow_ready = sem("iota_ready"), sem("zrow_ready")
        bias_ready, dve_step = sem("bias_ready"), sem("dve_step")
        ss_ready, var_ready, sd_ready, xs_ready = (sem(n) for n in ("ss_ready", "var_ready", "sd_ready", "xs_ready"))
        xT_filled, xT_ready = sem("xT_filled"), sem("xT_ready")
        xT_hi = sem("xT_hi")
        absap_ready, expap_ready, cc_ready = sem("absap_ready"), sem("expap_ready"), sem("cc_ready")
        xc_ready, rope_done = sem("xc_ready"), sem("rope_done")
        gates_filled, gates_read, tanh_done, a_ready = (sem(n) for n in (
            "gates_filled", "gates_read", "tanh_done", "a_ready"))
        zsig_ready, sxc_ready, a2_ready, m2_ready, mult_ready, gelu_ready, hg_ready, hghi_ready, hglo_ready = (
            sem(n) for n in ("zsig_ready", "sxc_ready", "a2_ready", "m2_ready", "mult_ready", "gelu_ready",
                             "hg_ready", "hghi_ready", "hglo_ready"))
        s_filled, negmax_ready, p_exp, p_ready = (sem(n) for n in (
            "s_filled", "negmax_ready", "p_exp", "p_ready"))
        pT_filled, pT_ready, o_filled, ohi_ready, o_ready = (sem(n) for n in (
            "pT_filled", "pT_ready", "o_filled", "ohi_ready", "o_ready"))
        mixr_done, mixsum_ready, mixhi_ready, mix_ready = (sem(n) for n in (
            "mixr_done", "mixsum_ready", "mixhi_ready", "mix_ready"))
        x1_ready, ss2_ready, var2_ready, sd2_ready, rstd2_ready, hn_ready = (sem(n) for n in (
            "x1_ready", "ss2_ready", "var2_ready", "sd2_ready", "rstd2_ready", "hn_ready"))
        x1T_filled, x1T_ready, x1T_last, rw_scaled, sel0_ready = (sem(n) for n in (
            "x1T_filled", "x1T_ready", "x1T_last", "rw_scaled", "sel0_ready"))
        part0_ready, rest_ready, part1_ready, parts_ready = (sem(n) for n in (
            "part0_ready", "rest_ready", "part1_ready", "parts_ready"))
        lg_filled, negm_ready, ex_ready, mask_ready, pos_filled, pos_ready = (sem(n) for n in (
            "lg_filled", "negm_ready", "ex_ready", "mask_ready", "pos_filled", "pos_ready"))
        gates_ready, count_ready, gT_filled, gT_ready, y_opened = (sem(n) for n in (
            "gates_ready", "count_ready", "gT_filled", "gT_ready", "y_opened"))
        sel_ready, gathered, xg_ready = sem("sel_ready"), sem("gathered"), sem("xg_ready")
        gu_used, dn_used, gu_read = sem("gu_used"), sem("dn_used"), sem("gu_read")
        wT_filled, wT_ready, glu_ready, sig_ready, t_ready, act_ready = (sem(n) for n in (
            "wT_filled", "wT_ready", "glu_ready", "sig_ready", "t_ready", "act_ready"))
        actT_filled, actT_ready, y_ready = sem("actT_filled"), sem("actT_ready"), sem("y_ready")
        moe_done, ss3_ready, var3_ready, sd3_ready, fin_ready = (sem(n) for n in (
            "moe_done", "ss3_ready", "var3_ready", "sd3_ready", "fin_ready"))

        w_gu_rows = w_gu.rearrange("l e k n -> (l e k) n")
        w_dn_rows = w_down.rearrange("l e k n -> (l e k) n")

        def overflow_passes(eng, body):
            eng.wait_ge(count_ready, 1)
            most = eng.value_load(cnt_i[0:1, 0:1], min_val=0, max_val=T)
            with eng.If(most > SLOTS):
                with eng.Fori(1, PASSES, 1) as p:
                    body(p)

        block = ctx.enter_context(nc.Block())

        @block.sync
        def _(sp):
            for t in range(TT):
                sp.dma_start(x_sb[:, t, :], x[0, t * P:(t + 1) * P, :]).then_inc(x_landed[t], 16)
            sp.dma_start(vec[:, :, :], vecs.rearrange("p (n k) -> p n k", n=N_VEC)).then_inc(vec_landed, 16)
            blocks = [w_in[0, :, c:c + 512] for c in range(0, 7 * D, 512)]
            for w in (w_proj_rnn, w_proj_attn, w_out):
                blocks += [w[0, :, 0:512], w[0, :, 512:1024]]

            def load_gu(row, par, wait, ks=range(KT)):
                for k in ks:
                    wait(k)
                    sp.dma_start(gu[par][k][:, :], w_gu_rows[ds(row + k * P, P), :]).then_inc(gu_landed[par][k], 16)

            def load_dn(row, wait, js=range(4)):
                for j in js:
                    wait(j)
                    src = w_dn_rows[ds(row + j * 2 * P, 2 * P), :].rearrange("(k p) n -> p k n", p=P)
                    if j < 3:
                        sp.dma_start(dn[j][:, :, :], src).then_inc(dn_landed[j], 16)
                    else:
                        for c in range(2):
                            sp.dma_start(dn[j][:, c, :], src[:, c, :]).then_inc(dn_landed[j + c], 16)

            for u, src in enumerate(blocks):
                if u >= LAND:
                    sp.wait_ge(lo_ready, PIECES * (u - LAND + 1))
                src = src.rearrange("(k p) n -> p k n", p=P)
                if u == 0:
                    sp.dma_start(land[0][:, :, 0:256], src[:, :, 0:256]).then_inc(first_landed, 16)
                    sp.dma_start(land[0][:, :, 256:512], src[:, :, 256:512]).then_inc(w_landed[0], 16)
                else:
                    sp.dma_start(land[u % LAND][:, :, :], src).then_inc(w_landed[u % LAND], 16)
                if u == 1:
                    for q in range(3):
                        sp.dma_start(b96[32 * q:32 * q + 32, :], b_gu[0]).then_inc(b96_landed, 16)
                    sp.wait_ge(bd_zeroed, 1)
                    for w, bd, landed in ((lru_wx, wx_bd, wx_landed), (lru_wa, wa_bd, wa_landed)):
                        for odd in range(2):
                            src = w[0].rearrange("(j o) i k -> o i j k", o=2)[odd]
                            sp.dma_start(bd[64 * odd:64 * odd + 64, :, 64 * odd:64 * odd + 64], src).then_inc(
                                landed, 16)
                    sp.dma_start(cos_t[:, :], rope[0]).then_inc(rope_landed, 16)
                    sp.dma_start(sin_t[:, :], rope[1]).then_inc(rope_landed, 16)
                    sp.dma_start(rw[:, :, :], router_w[0].rearrange("(k p) e -> p k e", p=P)).then_inc(rw_landed, 16)
                    sp.dma_start(rbb[:, :], router_b[0:1, :].to_broadcast([P, N_E])).then_inc(rbb_landed, 16)
                for i, (z, after) in enumerate(((z_q, 7), (z_k, 9))):
                    if u == after:
                        sp.wait_ge(evicted, 4 + (12, 16)[i])
                        for half in range(2):
                            sp.dma_start(rot[i][16 * half:16 * half + 16, :, :],
                                         z[16 * (1 - half):16 * (1 - half) + 16, :, :]).then_inc(rot_landed[i], 16)
                if u == 17:
                    sp.wait_ge(filled, 29)
                    for q in range(4):
                        sp.dma_start(bdn4[32 * q:32 * q + 32, :], b_down[0, :, (q % 2) * HALF:(q % 2 + 1) * HALF]
                                     ).then_inc(bdn_landed, 16)

                if u == 11:
                    load_gu(D, 1, lambda k: sp.wait_ge(b96_landed, 48), [3])
                if u == 12:
                    load_gu(D, 1, lambda k: sp.wait_ge(hglo_ready, 1), [5])
                if u == 13:
                    load_dn(0, lambda j: sp.wait_ge(hg_ready, 1), [3, 2])
                if u in (14, 15):
                    load_gu(D, 1, lambda k: sp.wait_ge(s_filled, H), [u - 14])
                if u == 16:
                    load_gu(D, 1, lambda k: sp.wait_ge(filled, 28), [2])
                if u == 18:
                    load_dn(0, lambda j: sp.wait_ge(filled, 32), [1])
            load_dn(0, lambda j: sp.wait_ge(filled, 36), [0])
            load_gu(D, 1, lambda k: sp.wait_ge(filled, 36), [4])
            load_gu(D, 1, lambda k: sp.wait_ge(mix_ready, 4), [6, 7])
            load_gu(0, 0, lambda k: sp.wait_ge(lo_ready, 76 if k < 2 else 80), range(0, 3))
            load_gu(0, 0, lambda k: sp.wait_ge(filled, 39), [4, 6])
            load_gu(0, 0, lambda k: sp.wait_ge(filled, 40), [5, 7])
            load_gu(0, 0, lambda k: sp.wait_ge(lg_filled, 1), [3])

            def load_pair(E, row):
                load_gu(row, 0, lambda k: sp.wait_ge(gu_used, KT * E + (k + 1 - 2 * KT)))
                load_dn(row, lambda j: sp.wait_ge(dn_used, 4 * E + (j + 1 - 4)))
                load_gu(row + D, 1, lambda k: sp.wait_ge(gu_used, KT * E + (k + 1 - KT)))
                load_dn(row + D, lambda j: sp.wait_ge(dn_used, 4 * E + (j + 1)))

            with sp.Fori(1, TURN, 1) as i:
                load_gu(i * (2 * D), 0, lambda k: sp.wait_ge(gu_used, KT * (2 * i) + (k + 1 - 2 * KT)))
                load_dn(i * (2 * D) - D, lambda j: sp.wait_ge(dn_used, 8 * i + (j + 1 - 8)))
                load_gu(i * (2 * D) + D, 1, lambda k: sp.wait_ge(gu_used, KT * (2 * i) + (k + 1 - KT)))
                load_dn(i * (2 * D), lambda j: sp.wait_ge(dn_used, 8 * i + (j + 1 - 4)))
            load_dn((2 * TURN - 1) * D, lambda j: sp.wait_ge(dn_used, 8 * TURN + (j + 1 - 8)))
            with sp.Fori(TURN, N_E // 2, 1) as i:
                load_pair(2 * i, i * (2 * D))

            def again(p):
                with sp.Fori(0, N_E // 2, 1) as i:
                    load_pair(p * N_E + 2 * i, i * (2 * D))

            overflow_passes(sp, again)
            for t in range(TT):
                sp.wait_ge(fin_ready, t + 1)
                sp.dma_start(out[0, t * P:(t + 1) * P, :], fin[:, t, :]).then_inc(out_landed, 16)
            sp.wait_ge(out_landed, 16 * TT)

        @block.gpsimd
        def _(pool):
            steps = [0]

            def link(ins):
                steps[0] += 1
                ins.then_inc(pool_step, 1)
                pool.wait_ge(pool_step, steps[0])

            link(pool.memset(ident[:, :], 0.0))
            pool.affine_select(out=ident[:, :], in_=ident[:, :], compare_op=ALU.not_equal, fill=1.0, base=0,
                               pattern=[[-1, P]], channel_multiplier=1).then_inc(consts_ready, 1)
            pool.memset(wx_bd[:, :, :], 0.0)
            pool.memset(wa_bd[:, :, :], 0.0).then_inc(bd_zeroed, 1)
            link(pool.memset(causal[:, :], 0.0))
            link(pool.affine_select(out=causal[:, :], in_=causal[:, :], compare_op=ALU.is_ge, fill=NEG, base=0,
                                    pattern=[[-1, P]], channel_multiplier=1))
            link(pool.memset(ones[:, :], 1.0))
            pool.affine_select(out=tri[:, :], in_=ones[:, :], compare_op=ALU.is_ge, fill=0.0, base=-1,
                               pattern=[[1, P]], channel_multiplier=-1).then_inc(consts_ready, 1)

            with pool.Fori(0, N_BLK // LAND, 1) as it:
                for q in range(PIECES * LAND):
                    pool.wait_ge(hi_ready, PIECES * LAND * it + (q + 1))
                    pool.tensor_tensor(w_lo[:, q % PIECES], land[q // PIECES][:, :, (q % PIECES) * P:(q % PIECES + 1) * P],
                                       w_hi[:, q % PIECES].bitcast(f32), ALU.subtract).then_inc(lo_ready, 1)
            pool.memset(zrow[:, :], 0.0).then_inc(zrow_ready, 1)
            link(pool.iota(iota[:, :], pattern=[[1, SLOTS]], base=1, channel_multiplier=0,
                           allow_small_or_imprecise_dtypes=True))
            link(pool.memset(ident3[:, :], 0.0))
            for third in range(3):
                ins = pool.affine_select(out=ident3[:, :], in_=ident3[:, :], compare_op=ALU.not_equal, fill=1.0,
                                         base=-32 * third, pattern=[[-1, N_E + 1]], channel_multiplier=1)
                if third < 2:
                    link(ins)
            ins.then_inc(iota_ready, 1)
            pool.wait_ge(y_opened, 1)
            pool.wait_ge(hn_ready, TT)
            pool.dma_start(gfin[:, :], norm_final_g.rearrange("(o n) -> o n", o=1).to_broadcast([P, D])).then_inc(
                gfin_landed, 16)

        @block.tensor
        def _(pe):
            mm = nc.tensor.matmul

            def keep_clock(bank, n):
                for _ in range(n):
                    mm(ps[:, bank, :], ones[:, :], ones[:, :].unsqueeze(1).to_broadcast([P, 4, P]),
                       start=True, stop=True)

            pe.wait_ge(consts_ready, 1)
            for _ in range(WARM):
                nc.tensor.transpose(ps[:, 0, 0:P], ident[:, :], ident[:, :])
            for t in range(TT):
                pe.wait_ge(xs_ready, t + 1)
                for k in range(KT):
                    last = nc.tensor.transpose(ps[:, 4 + k // 2, (k % 2) * T + t * P:(k % 2) * T + (t + 1) * P],
                                               xs[:, t, k * P:(k + 1) * P], ident[:, :])
                    if t == TT - 1 and k % 2 == 1:
                        last.then_inc(xT_filled, 1)
            def transposed(h, bank, src_hi, src_lo, base=0, first=False):
                for c in range(2):
                    b = (2 * h + c) % PIECES
                    to = ps[:, bank, c * T:(c + 1) * T]
                    pe.wait_ge(hi_ready, base + (2 * h + c + 1))
                    for k in range(KT):
                        if first and c == 0:
                            pe.wait_ge(xT_ready, k + 1)
                        mm(to, w_hi[:, b, k, :], src_hi[:, k, :], start=k == 0, stop=False)
                        mm(to, w_hi[:, b, k, :], src_lo[:, k, :], start=False, stop=False)
                    pe.wait_ge(lo_ready, base + (2 * h + c + 1))
                    for k in range(KT):
                        last = mm(to, w_lo[:, b, k, :], src_hi[:, k, :], start=False, stop=k == KT - 1)
                last.then_inc(filled, 1)

            def natural(h, bank, src_hi, src_lo, mixing=False):
                b = (2 * h) % PIECES
                for t in range(TT):
                    to = ps[:, bank, t * T:(t + 1) * T].rearrange("p (c n) -> p c n", c=2)
                    rows = slice(t * P, (t + 1) * P)
                    if t == 0:
                        pe.wait_ge(hi_ready, 2 * h + 2)
                    early = KT - 2 if mixing and t == 0 else KT
                    for k in range(early):
                        if mixing and t == 0 and k % 2 == 0:
                            pe.wait_ge(mix_ready, k // 2 + 1)
                        mm(to, src_hi[:, k, rows], w_hi[:, b:b + 2, k, :], start=k == 0, stop=False)
                        mm(to, src_lo[:, k, rows], w_hi[:, b:b + 2, k, :], start=False, stop=False)
                    if t == 0:
                        pe.wait_ge(lo_ready, 2 * h + 2)
                    for k in range(early):
                        last = mm(to, src_hi[:, k, rows], w_lo[:, b:b + 2, k, :], start=False, stop=k == KT - 1)
                    if early < KT:
                        pe.wait_ge(mixhi_ready, 4)
                        for k in range(early, KT):
                            mm(to, src_hi[:, k, rows], w_hi[:, b:b + 2, k, :], start=False, stop=False)
                            mm(to, src_hi[:, k, rows], w_lo[:, b:b + 2, k, :], start=False, stop=False)
                        pe.wait_ge(mix_ready, 4)
                        for k in range(early, KT):
                            mm(to, src_lo[:, k, rows], w_hi[:, b:b + 2, k, :], start=False, stop=k == KT - 1)
                last.then_inc(filled, 1)

            def z_halves(first):
                with pe.Fori(0, 2, 1) as it:
                    for h in range(first, first + 4):
                        pe.wait_ge(evicted, 4 * it + (h + 1))
                        transposed(h, h % 4, x_hi, x_lo, base=8 * it, first=h == 0)

            z_halves(0)
            pe.wait_ge(wx_landed, 32)
            pe.wait_ge(wa_landed, 32)
            for j in range(KT):
                pe.wait_ge(xc_ready, j + 1)
                if j >= 4:
                    pe.wait_ge(gates_read, j - 3)
                b = 4 + j % 4
                mm(ps[:, b, 0:T], wx_bd[:, j, :], xc[:, j, :], start=True, stop=True)
                mm(ps[:, b, T:2 * T], wa_bd[:, j, :], xc[:, j, :], start=True, stop=True).then_inc(gates_filled, 1)
            z_halves(8)
            def scores(i):
                if i == 0:
                    pe.wait_ge(rope_done, 2)
                    pe.wait_ge(gates_read, KT)
                if i >= 2:
                    pe.wait_ge(negmax_ready, i - 1)
                q, k = z_q[:, i, :], z_k[:, i, :]
                mm(ps[:, 4 + i % 2, 0:P], q[:, 0:P], k[:, 0:P], start=True, stop=True)
                mm(ps[:, 4 + i % 2, P:384], q[:, P:T], k, start=True, stop=True).then_inc(s_filled, 1)

            def transpose_p(i):
                pe.wait_ge(p_ready, i + 1)
                if i >= 1:
                    pe.wait_ge(pT_ready, i)
                for c in range(3):
                    last = nc.tensor.transpose(ps[:, 6, c * P:(c + 1) * P], s_sb[i % 2][:, c * P:(c + 1) * P],
                                               ident[:, :])
                last.then_inc(pT_filled, 1)

            def times_v(i):
                pe.wait_ge(pT_ready, i + 1)
                if i == 0:
                    pe.wait_ge(evicted, 4 + 20)
                if i >= 1:
                    pe.wait_ge(o_ready, i)
                v0, v1 = (v_sb[:, t, i * P:(i + 1) * P] for t in range(TT))
                o = ps[:, 7, 0:T]
                mm(o[:, 0:P], v0, pT[i % 2][:, 0:P], start=True, stop=True)
                mm(o[:, P:T], v0, pT[i % 2][:, P:T], start=True, stop=False)
                mm(o[:, P:T], v1, pT[i % 2][:, T:384], start=False, stop=True).then_inc(o_filled, 1)

            for h in range(16, 20):
                if h == 19:
                    scores(0)
                    scores(1)
                pe.wait_ge(evicted, h + 1)
                natural(h, h % 4, x_hi, x_lo)
            for i in range(H):
                h = 20 + i
                pe.wait_ge(evicted, h + 1)
                transposed(h, h % 4, x_hi, x_lo)
                transpose_p(i)
                if i + 2 < H:
                    scores(i + 2)
                if i >= 1:
                    times_v(i - 1)
            pe.wait_ge(hglo_ready, 1)
            for h in range(28, 32):
                pe.wait_ge(evicted, h + 1)
                transposed(h, h % 4, hg_hi, hg_lo)
                if h == 28:
                    times_v(H - 1)
            pe.wait_ge(o_ready, H)
            for h in range(32, 36):
                transposed(h, 4 + h % 4, o_hi, o_lo)
            def transpose_x1(n):
                pe.wait_ge(x1_ready, n + 1)
                for c in range(2):
                    for t in range(TT):
                        last = nc.tensor.transpose(ps[:, 4 + n, c * T + t * P:c * T + (t + 1) * P],
                                                   x_sb[:, t, (2 * n + c) * P:(2 * n + c + 1) * P], ident[:, :])
                last.then_inc(x1T_filled, 1)

            def logits(n):
                if n < 3:
                    pe.wait_ge(x1T_ready, max(n + 1, TT))
                else:
                    pe.wait_ge(x1T_last, 1)
                for t in range(TT):
                    for k in (2 * n, 2 * n + 1):
                        last = mm(ps[:, 4 + t, 0:N_E], x1T[:, k, t * P:(t + 1) * P], rw[:, k, :],
                                  start=n == 0 and k == 0, stop=n == 3 and k == KT - 1)
                if n == 3:
                    last.then_inc(lg_filled, 1)

            for n in range(4):
                pe.wait_ge(mixr_done, n + 1)
                natural(36 + n, n, mix_hi, mix_lo, mixing=n == 0)
                if n >= 1:
                    transpose_x1(n - 1)
                if n == 1:
                    pe.wait_ge(rw_scaled, 1)
            logits(0)
            transpose_x1(3)
            logits(1)
            logits(2)

            def open_y(t):
                for h in range(2):
                    last = mm(ps[:, 2 * t + h, :], ident[:, :], x_sb[:, t, h * HALF:(h + 1) * HALF],
                              start=True, stop=False)
                last.then_inc(y_opened, 1)

            logits(3)
            pe.wait_ge(zrow_ready, 1)
            keep_clock(3, 5)
            pe.wait_ge(mask_ready, 1)
            mm(ps[:, 7, 0:N_E], tri[:, :], maskb[:, 0, :], start=True, stop=True)
            mm(ps[:, 7, N_E:2 * N_E], ones[:, :], maskb[:, 0, :], start=True, stop=False)
            mm(ps[:, 7, N_E:2 * N_E], tri[:, :], maskb[:, 1, :], start=False, stop=True)
            mm(ps[:, 7, 64:96], ones[:, :], maskb[:, 0, :], start=True, stop=False)
            mm(ps[:, 7, 64:96], ones[:, :], maskb[:, 1, :], start=False, stop=True).then_inc(pos_filled, 1)
            keep_clock(3, 3)

            def gather(buf):
                for k in range(KT):
                    for n, (t, q) in enumerate((t, q) for t in range(TT) for q in range(3)):
                        last = mm(ps[:, 6, k * SLOTS:(k + 1) * SLOTS], part[q][:, t, k * P:(k + 1) * P],
                                  sel[buf][:, t, :], start=n == 0, stop=n == 3 * TT - 1)
                last.then_inc(gathered, 1)

            pe.wait_ge(sel0_ready, 1)
            pe.wait_ge(hn_ready, TT)
            for half in range(2):
                if half == 1:
                    pe.wait_ge(count_ready, 1)
                for j in range(4):
                    k = 4 * half + j
                    for t in range(TT):
                        last = mm(ps[:, 6 + half, j * SLOTS:(j + 1) * SLOTS], hn[:, t, k * P:(k + 1) * P],
                                  sel0[:, t, :], start=t == 0, stop=t == TT - 1)
                last.then_inc((gathered_half, gathered)[half], 1)
            pe.wait_ge(bias_ready, 2)

            def add_b_down():
                pe.wait_ge(gates_ready, 1)
                for t in range(TT):
                    last = nc.tensor.transpose(ps[:, 7, t * P:(t + 1) * P], gates4[:, t], ident[:, :])
                last.then_inc(gT_filled, 1)
                pe.wait_ge(gT_ready, 1)
                pe.wait_ge(bdn_landed, 64)
                for q in range(4):
                    t, rows = q // 2, slice(32 * q, 32 * q + 32)
                    mm(ps[:, q, :], gT4[rows, t * P:(t + 1) * P], bdn4[rows, :], start=False, stop=False)

            def expert(E, X, par, meanwhile=None, first=False):
                if first:
                    pe.wait_ge(xg_half, 1)
                else:
                    pe.wait_ge(xg_ready, X + (par + 1))
                pe.wait_ge(gu_read, E + (par + 1))
                for c in range(2):
                    for h in range(2):
                        mm(ps[64 * h:64 * h + 64, 4 + c, :], bsel[par][:, :],
                           bias3[:, c * D + h * HALF:c * D + (h + 1) * HALF], start=True, stop=False)
                for k in range(KT):
                    pe.wait_ge(gu_landed[par][k], 8 * E + 16)
                    if first and k == 4:
                        pe.wait_ge(xg_ready, 1)
                    for c in range(2):
                        for h in range(2):
                            last = mm(ps[64 * h:64 * h + 64, 4 + c, :], xg[:, k * SLOTS:(k + 1) * SLOTS],
                                      gu[par][k][:, c * D + h * HALF:c * D + (h + 1) * HALF],
                                      start=False, stop=k == KT - 1)
                    last.then_inc(gu_used, 1)
                pe.wait_ge(parts_ready, TT)
                pe.wait_ge(sel_ready, X + (par + 1))
                for t in range(TT):
                    last = nc.tensor.transpose(ps[:, 7, t * P:(t + 1) * P], sel_g[par][:, t, :], ident[:, :])
                last.then_inc(wT_filled, 1)
                pe.wait_ge(sel_ready, X + (par + 2))
                gather(1 - par)
                pe.wait_ge(wT_ready, E + (par + 1))
                if meanwhile:
                    meanwhile()
                if not meanwhile:
                    keep_clock(7, 5)
                pe.wait_ge(act_ready, E + (par + 1))
                for j in range(4):
                    last = nc.tensor.transpose(ps[:, 7, j * P:(j + 1) * P], act_s[:, j * P:(j + 1) * P], ident[:, :])
                last.then_inc(actT_filled, 1)
                keep_clock(4, 3)
                pe.wait_ge(actT_ready, E + (par + 1))
                pe.wait_ge(xg_ready, X + (par + 2))
                for k in range(KT):
                    if k % 2 == 0 or k == KT - 1:
                        pe.wait_ge(dn_landed[(k + 1) // 2], 16 * E + 16 * (par + 1))
                    for h in range(2):
                        last = mm(ps[64 * h:64 * h + 64, 6, :], actT[:, k % 4, (k // 4) * SLOTS:(k // 4 + 1) * SLOTS],
                                  dn[k // 2][:, k % 2, h * HALF:(h + 1) * HALF], start=k == 0, stop=k == KT - 1)
                    if k % 2 == 1:
                        last.then_inc(dn_used, 1)
                pe.wait_ge(y_ready, E + (par + 1))
                for t in range(TT):
                    for h in range(2):
                        mm(ps[:, 2 * t + h, :], wT[64 * h:64 * h + 64, t * P:(t + 1) * P], y_sb[64 * h:64 * h + 64, :],
                           start=False, stop=False)

            expert(0, 0, 0, lambda: (open_y(0), open_y(1)), first=True)
            expert(0, 0, 1, add_b_down)
            with pe.Fori(1, N_E // 2, 1) as i:
                for par in range(2):
                    expert(2 * i, 2 * i, par)

            def again(p):
                pe.wait_ge(sel_ready, PER_PASS * p + 1)
                gather(0)
                with pe.Fori(0, N_E // 2, 1) as i:
                    for par in range(2):
                        expert(p * N_E + 2 * i, p * PER_PASS + 2 * i, par)

            overflow_passes(pe, again)
            for b in range(4):
                last = mm(ps[:, b, :], zrow[0:1, :], ones[0:1, :].unsqueeze(1).to_broadcast([1, 4, P]),
                          start=False, stop=True)
                if b % 2 == 1:
                    last.then_inc(moe_done, 1)

        @block.scalar
        def _(act):
            A = nc.scalar.activation
            act.wait_ge(spare_ready, 1)
            A(spare, spare, ACT.Sqrt)
            for t in range(TT):
                act.wait_ge(x_landed[t], 16)
                A(xc[:, 4 * t:4 * t + 4, :], x_sb[:, t, :].rearrange("p (c t) -> p c t", c=4), ACT.Square,
                  accum_out=ss[:, t:t + 1]).then_inc(ss_ready, 1)
                act.wait_ge(var_ready, t + 1)
                A(rstd[:, t:t + 1], rstd[:, t:t + 1], ACT.Sqrt).then_inc(sd_ready, 1)

            def split_hi(q):
                u = q // PIECES
                if q == 0:
                    act.wait_ge(first_landed, 16)
                if q == 2 or q > 2 and q % PIECES == 0:
                    act.wait_ge(w_landed[u % LAND], 16 * (u // LAND + 1))
                if q >= PIECES:
                    act.wait_ge(filled, (q - PIECES) // 2 + 1)
                A(w_hi[:, q % PIECES], land[u % LAND][:, :, (q % PIECES) * P:(q % PIECES + 1) * P],
                  ACT.Copy).then_inc(hi_ready, 1)

            v_quarter = v_sb[:, :, :].rearrange("p t (c n) -> p c t n", c=4)

            def evict(h):
                act.wait_ge(filled, h + 1)
                bank = ps[:, h % 4, :].rearrange("p (c t) -> p c t", c=2)
                if 16 <= h < 20:
                    to = v_quarter[:, h - 16]
                else:
                    z = (z_x, z_gate, z_q, z_k, None, z_gr, z_ga)[h // 4]
                    to = z[:, 2 * (h % 4):2 * (h % 4) + 2, :]
                A(to, bank, ACT.Copy).then_inc(evicted, 1)

            def turn(h):
                if h < 8:
                    evict(h)
                if h + 2 < 2 * N_BLK:
                    split_hi(2 * h + 4)
                    split_hi(2 * h + 5)
                if 8 <= h < 28:
                    evict(h)

            split_hi(0)
            act.wait_ge(vec_landed, 16)
            for k in range(KT):
                if k % 2 == 0:
                    act.wait_ge(xT_filled, k // 2 + 1)
                A(x_hi[:, k, :], ps[:, 4 + k // 2, (k % 2) * T:(k % 2 + 1) * T], ACT.Copy,
                  scale=vec[:, V_GMIX, k:k + 1]).then_inc(xT_hi, 1)
            for q in range(1, PIECES):
                split_hi(q)
            act.wait_ge(absap_ready, 1)
            A(spu, spu, ACT.Exp, scale=-1.0).then_inc(expap_ready, 1)
            for _ in range(4):
                act.nop().then_inc(evicted, 1)
            for h in range(8):
                if h == 7:
                    A(spare, spare, ACT.Sigmoid)
                turn(h)
            for j in range(KT):
                act.wait_ge(gates_filled, j + 1)
                A(sx[:, j, :], ps[:, 4 + j % 4, 0:T], ACT.Sigmoid, bias=vec[:, V_BX, j:j + 1])
                A(sa[:, j, :], ps[:, 4 + j % 4, T:2 * T], ACT.Sigmoid, bias=vec[:, V_BA, j:j + 1]).then_inc(
                    gates_read, 1)
            act.wait_ge(cc_ready, 1)
            act.wait_ge(gates_read, KT)
            for h in range(8, 12):
                turn(h)
                for j in range(2 * (h - 8), 2 * (h - 8) + 2):
                    A(th[:, j, :], sa[:, j, :], ACT.Tanh, scale=cpos[:, j:j + 1]).then_inc(tanh_done, 1)
            act.wait_ge(tanh_done, KT)
            for h in range(12, 14):
                turn(h)
                for j in range(4 * (h - 12), 4 * (h - 12) + 4):
                    A(sa[:, j, :], sa[:, j, :], ACT.Exp, scale=cneg[:, j:j + 1]).then_inc(a_ready, 1)
            turn(14)
            act.wait_ge(sxc_ready, 1)
            act.wait_ge(a_ready, KT)
            A(xc[:, :, :], sa[:, :, :], ACT.Square).then_inc(a2_ready, 1)
            turn(15)
            act.wait_ge(evicted, 4 + 8)
            A(z_gate[:, :, :], z_gate[:, :, :], ACT.Gelu_apprx_tanh).then_inc(gelu_ready, 1)
            turn(16)
            act.wait_ge(m2_ready, 1)
            A(th[:, :, :], th[:, :, :], ACT.Sqrt).then_inc(mult_ready, 1)
            turn(17)
            A(spare, spare, ACT.Exp)
            act.wait_ge(hg_ready, 1)
            A(hg_hi[:, :, :], z_gate[:, :, :], ACT.Copy).then_inc(hghi_ready, 1)
            turn(18)
            turn(19)

            def exps(i):
                act.wait_ge(negmax_ready, i + 1)
                s = s_sb[i % 2]
                A(s[:, 0:P], s[:, 0:P], ACT.Exp, bias=mx[:, i % 2, 0:1], scale=SCALE, accum_out=sm[:, i % 2, 0:1])
                A(s[:, P:384], s[:, P:384], ACT.Exp, bias=mx[:, i % 2, 1:2], scale=SCALE,
                  accum_out=sm[:, i % 2, 1:2]).then_inc(p_exp, 1)

            def keep_pT(i):
                act.wait_ge(pT_filled, i + 1)
                if i >= 2:
                    act.wait_ge(o_filled, i - 1)
                A(pT[i % 2][:, :], ps[:, 6, 0:384], ACT.Copy).then_inc(pT_ready, 1)

            def keep_o(i):
                act.wait_ge(o_filled, i + 1)
                A(o_hi[:, i, :], ps[:, 7, 0:T], ACT.Copy).then_inc(ohi_ready, 1)

            exps(0)
            for i in range(1, H + 1):
                keep_pT(i - 1)
                turn(19 + i)
                if i >= 2:
                    keep_o(i - 2)
                if i < H:
                    exps(i)
            act.wait_ge(evicted, 4 + 28)
            A(z_gr[:, :, :], z_gr[:, :, :], ACT.Sigmoid).then_inc(zsig_ready, 1)
            turn(28)
            keep_o(H - 1)
            A(z_ga[:, :, :], z_ga[:, :, :], ACT.Sigmoid).then_inc(zsig_ready, 1)
            for h in range(29, 38):
                if h != 35:
                    turn(h)
                if h >= 32 and h < 36:
                    j = h - 32
                    act.wait_ge(mixsum_ready, j + 1)
                    A(mix_hi[:, 2 * j:2 * j + 2, :], z_ga[:, 2 * j:2 * j + 2, :], ACT.Copy).then_inc(mixhi_ready, 1)
                if h == 35:
                    turn(h)
            A(spare, spare, ACT.Sqrt)
            for n in range(4):
                act.wait_ge(x1_ready, n + 1)
                for t in range(TT):
                    A(sq_out[:, n, t, :], x_sb[:, t, n * T:(n + 1) * T], ACT.Square,
                      accum_out=ss2p[:, t, n:n + 1]).then_inc(ss2_ready, 1)
                if n < 3:
                    act.wait_ge(x1T_filled, n + 1)
                    act.wait_ge(lo_ready, 4 * N_BLK)
                    A(x1T[:, 2 * n:2 * n + 2, :], ps[:, 4 + n, :].rearrange("p (c t) -> p c t", c=2),
                      ACT.Copy).then_inc(x1T_ready, 1)
            act.wait_ge(var2_ready, 1)
            A(rstd2, rstd2, ACT.Sqrt).then_inc(sd2_ready, 1)
            act.wait_ge(rstd2_ready, 1)
            A(hn[:, 1, :], x_sb[:, 1, :], ACT.Copy, scale=rstd2[:, 1:2]).then_inc(hn_ready, 1)
            act.wait_ge(negm_ready, 1)
            for t in range(TT):
                A(ex[:, t, :], lg[:, t, 0:N_E], ACT.Exp, bias=negm[:, t:t + 1]).then_inc(ex_ready, 1)
            act.wait_ge(hn_ready, TT)
            for t in range(TT):
                A(part[0][:, t, :], hn[:, t, :], ACT.Copy).then_inc(part0_ready, 1)
            for t in range(TT):
                act.wait_ge(rest_ready, t + 1)
                A(part[1][:, t, :], hn[:, t, :], ACT.Copy).then_inc(part1_ready, 1)
            A(spare, spare, ACT.Sigmoid)

            def expert(E, par, meanwhile=None):
                act.wait_ge(wT_filled, E + (par + 1))
                A(wT[:, :], ps[:, 7, 0:T], ACT.Copy).then_inc(wT_ready, 1)
                act.wait_ge(glu_ready, E + (par + 1))
                A(act_s[:, :], g1[:, :], ACT.Sigmoid, scale=ALPHA).then_inc(sig_ready, 1)
                if meanwhile:
                    meanwhile()
                act.wait_ge(dn_used, 4 * E + 4 * (par + 1))
                A(y_sb[:, :], ps[:, 6, :], ACT.Copy).then_inc(y_ready, 1)

            def keep_gates():
                act.wait_ge(gT_filled, 1)
                A(gT4[:, :], ps[:, 7, 0:T], ACT.Copy).then_inc(gT_ready, 1)

            expert(0, 0)
            expert(0, 1, keep_gates)
            with act.Fori(1, N_E // 2, 1) as i:
                for par in range(2):
                    expert(2 * i, par)

            def again(p):
                with act.Fori(0, N_E // 2, 1) as i:
                    for par in range(2):
                        expert(p * N_E + 2 * i, par)

            overflow_passes(act, again)
            A(spare, spare, ACT.Sqrt)
            for t in range(TT):
                act.wait_ge(moe_done, t + 1)
                A(squares[:, t, :].rearrange("p (h n) -> p h n", h=2), ps[:, 2 * t:2 * t + 2, :], ACT.Square,
                  accum_out=ss3[:, t:t + 1]).then_inc(ss3_ready, 1)
                act.wait_ge(var3_ready, t + 1)
                A(rstd3[:, t:t + 1], rstd3[:, t:t + 1], ACT.Sqrt).then_inc(sd3_ready, 1)

        @block.vector
        def _(dve):
            V = nc.vector
            steps = [0]

            def link(ins):
                steps[0] += 1
                ins.then_inc(dve_step, 1)
                dve.wait_ge(dve_step, steps[0])

            def rsqrt_mean(total, r, t, summed, var):
                dve.wait_ge(summed, t + 1)
                V.tensor_scalar(r[:, t:t + 1], total[:, t:t + 1], 1.0 / D, EPS, ALU.mult, ALU.add).then_inc(var, 1)

            def reciprocal_of(r, t, sd):
                dve.wait_ge(sd, t + 1)
                link(V.reciprocal(r[:, t:t + 1], r[:, t:t + 1]))

            V.memset(spare, 1.0).then_inc(spare_ready, 1)
            for t in range(TT):
                rsqrt_mean(ss, rstd, t, ss_ready, var_ready)
                reciprocal_of(rstd, t, sd_ready)
                V.tensor_scalar(xs[:, t, :], x_sb[:, t, :], rstd[:, t:t + 1], None, ALU.mult).then_inc(xs_ready, 1)
            dve.wait_ge(vec_landed, 16)
            ap = vec[:, V_AP, :]
            V.scalar_tensor_tensor(out=spu, in0=ap, scalar=-1.0, in1=ap, op0=ALU.mult, op1=ALU.max).then_inc(
                absap_ready, 1)
            for k in range(KT):
                if k % 2 == 0:
                    dve.wait_ge(xT_hi, k + 2)
                V.scalar_tensor_tensor(out=x_lo[:, k, :], in0=ps[:, 4 + k // 2, (k % 2) * T:(k % 2 + 1) * T],
                                       scalar=vec[:, V_GMIX, k:k + 1], in1=x_hi[:, k, :].bitcast(f32),
                                       op0=ALU.mult, op1=ALU.subtract).then_inc(xT_ready, 1)
            dve.wait_ge(expap_ready, 1)
            link(V.tensor_scalar(cpos, spu, 2.0, None, ALU.add))
            link(V.reciprocal(cpos, cpos))
            link(V.tensor_tensor(spu, spu, cpos, ALU.mult))
            link(V.tensor_tensor(cpos, spu, spu, ALU.mult))
            link(V.tensor_scalar(sp2, cpos, 1.0 / 19, None, ALU.mult))
            for n in (17, 15, 13, 11, 9, 7, 5, 3):
                link(V.scalar_tensor_tensor(out=sp2, in0=sp2, scalar=1.0 / n, in1=cpos, op0=ALU.add, op1=ALU.mult))
            link(V.scalar_tensor_tensor(out=sp2, in0=sp2, scalar=1.0, in1=spu, op0=ALU.add, op1=ALU.mult))
            link(V.tensor_scalar(spu, ap, -1.0, 0.0, ALU.mult, ALU.max))
            link(V.scalar_tensor_tensor(out=sp2, in0=sp2, scalar=2.0, in1=spu, op0=ALU.mult, op1=ALU.add))
            V.tensor_scalar(cpos, sp2, LRU_C, None, ALU.mult)
            V.tensor_scalar(cneg, sp2, -LRU_C, None, ALU.mult).then_inc(cc_ready, 1)
            dve.wait_ge(b96_landed, 48)
            link(V.tensor_copy(bias3[:, :], b96[:, :]))
            for q in (1, 2):
                for r in range(q, 3):
                    rows = slice(32 * r, 32 * r + 32)
                    link(V.tensor_tensor(b96[rows, :], b96[rows, :], bias3[rows, :], ALU.subtract))
                    link(V.tensor_copy(bias3[rows, :], b96[rows, :]))
            V.memset(gates[:, :, :], 0.0)
            V.memset(pos[:, :, :], 0.0).then_inc(bias_ready, 1)
            dve.wait_ge(rw_landed, 16)
            V.tensor_tensor(rw[:, :, :], rw[:, :, :], vec[:, V_GFFN, :].unsqueeze(2).to_broadcast([P, KT, N_E]),
                            ALU.mult).then_inc(rw_scaled, 1)
            for j in range(KT):
                if j % 2 == 0:
                    dve.wait_ge(evicted, 4 + j // 2 + 1)
                    if j == 0:
                        dve.wait_ge(ss_ready, TT)
                z = z_x[:, j, :]
                link(V.tensor_scalar(xc[:, j, :], z, vec[:, V_CONVW + 3, j:j + 1], vec[:, V_CONVB, j:j + 1],
                                     ALU.mult, ALU.add))
                for back in (1, 2, 3):
                    ins = V.scalar_tensor_tensor(out=xc[:, j, back:T], in0=z[:, 0:T - back],
                                                 scalar=vec[:, V_CONVW + 3 - back, j:j + 1], in1=xc[:, j, back:T],
                                                 op0=ALU.mult, op1=ALU.add)
                    if back < 3:
                        link(ins)
                    else:
                        ins.then_inc(xc_ready, 1)
            dve.wait_ge(gates_read, KT)
            V.tensor_tensor(sx[:, :, :], sx[:, :, :], xc[:, :, :], ALU.mult).then_inc(sxc_ready, 1)

            def over_heads(table):
                return table[:, :].unsqueeze(1).to_broadcast([ROPE, H, T])

            def rotate(i, z):
                dve.wait_ge(rot_landed[i], 32)
                z = z[0:ROPE, :, :]
                V.tensor_tensor(z, z, over_heads(cos_t), ALU.mult)
                link(V.tensor_tensor(rot[i][:, :, :], rot[i][:, :, :], over_heads(sin_t), ALU.mult))
                V.tensor_tensor(z, z, rot[i][:, :, :], ALU.add).then_inc(rope_done, 1)

            dve.wait_ge(rope_landed, 32)
            rotate(0, z_q)
            dve.wait_ge(a2_ready, 1)
            V.scalar_tensor_tensor(out=th[:, :, :], in0=xc[:, :, :], scalar=1.0, in1=th[:, :, :],
                                   op0=ALU.add, op1=ALU.mult).then_inc(m2_ready, 1)
            rotate(1, z_k)
            dve.wait_ge(sxc_ready, 1)
            dve.wait_ge(mult_ready, 1)
            link(V.tensor_tensor(sx[:, :, :], sx[:, :, :], th[:, :, :], ALU.mult))
            for j in range(KT):
                ins = V.tensor_tensor_scan(out=xc[:, j, :], data0=sa[:, j, :], data1=sx[:, j, :], initial=0.0,
                                           op0=ALU.mult, op1=ALU.add)
            link(ins)
            dve.wait_ge(gelu_ready, 1)
            V.tensor_tensor(z_gate[:, :, :], z_gate[:, :, :], xc[:, :, :], ALU.mult).then_inc(hg_ready, 1)
            dve.wait_ge(hghi_ready, 1)
            V.tensor_tensor(hg_lo[:, :, :], z_gate[:, :, :], hg_hi[:, :, :].bitcast(f32), ALU.subtract).then_inc(
                hglo_ready, 1)

            def mask_and_max(i):
                dve.wait_ge(s_filled, i + 1)
                if i >= 2:
                    dve.wait_ge(pT_filled, i - 1)
                b, s = ps[:, 4 + i % 2, :], s_sb[i % 2]
                V.tensor_copy(s[:, P:T], b[:, P:T])
                V.tensor_tensor(s[:, 0:P], b[:, 0:P], causal[:, :], ALU.add)
                link(V.tensor_tensor(s[:, T:384], b[:, T:384], causal[:, :], ALU.add))
                V.reduce_max(mx[:, i % 2, 0:1], s[:, 0:P], AX.X)
                link(V.reduce_max(mx[:, i % 2, 1:2], s[:, P:384], AX.X))
                V.tensor_scalar(mx[:, i % 2, :], mx[:, i % 2, :], -SCALE, None, ALU.mult).then_inc(negmax_ready, 1)
                dve.wait_ge(negmax_ready, i + 1)

            def normalise(i):
                dve.wait_ge(p_exp, i + 1)
                link(V.reciprocal(sm[:, i % 2, :], sm[:, i % 2, :]))
                s = s_sb[i % 2]
                V.tensor_scalar(s[:, 0:P], s[:, 0:P], sm[:, i % 2, 0:1], None, ALU.mult)
                V.tensor_scalar(s[:, P:384], s[:, P:384], sm[:, i % 2, 1:2], None, ALU.mult).then_inc(p_ready, 1)

            def keep_o(i):
                dve.wait_ge(ohi_ready, i + 1)
                V.tensor_tensor(o_lo[:, i, :], ps[:, 7, 0:T], o_hi[:, i, :].bitcast(f32), ALU.subtract).then_inc(
                    o_ready, 1)

            dve.wait_ge(consts_ready, 2)
            for i in range(H):
                mask_and_max(i)
                if i >= 2:
                    keep_o(i - 2)
                normalise(i)
            keep_o(H - 2)
            keep_o(H - 1)

            def two(t, k):
                return t[:, k:k + 2, :]

            def bank(b):
                return ps[:, b, :].rearrange("p (c t) -> p c t", c=2)

            dve.wait_ge(zsig_ready, 1)
            for j in range(4):
                dve.wait_ge(filled, 28 + j + 1)
                V.tensor_tensor(two(z_gr, 2 * j), two(z_gr, 2 * j), bank(j), ALU.mult).then_inc(mixr_done, 1)
            dve.wait_ge(zsig_ready, 2)
            dve.wait_ge(mixr_done, 4)
            for j in range(4):
                z = two(z_ga, 2 * j)
                dve.wait_ge(filled, 32 + j + 1)
                link(V.tensor_tensor(z, z, bank(4 + j), ALU.mult))
                V.tensor_tensor(z, z, two(z_gr, 2 * j), ALU.add).then_inc(mixsum_ready, 1)
                dve.wait_ge(mixhi_ready, j + 1)
                V.tensor_tensor(two(mix_lo, 2 * j), z, two(mix_hi, 2 * j).bitcast(f32), ALU.subtract).then_inc(
                    mix_ready, 1)
            for n in range(4):
                dve.wait_ge(filled, 36 + n + 1)
                quarter = x_sb[:, :, n * T:(n + 1) * T]
                V.tensor_tensor(quarter, quarter, bank(n), ALU.add).then_inc(x1_ready, 1)
            dve.wait_ge(mix_ready, 4)
            dve.wait_ge(filled, 40)
            V.memset(lg[:, :, N_E:36], LOW)
            V.memset(v8[:, :, TOP_K:8], LOW)
            dve.wait_ge(iota_ready, 1)
            V.tensor_copy(bsel[0][:, :], ident3[:, 0:1].to_broadcast([96, SLOTS])).then_inc(bias_ready, 1)
            dve.wait_ge(x1T_filled, 4)
            V.tensor_copy(x1T[:, 6:8, :], bank(7)).then_inc(x1T_last, 1)
            dve.wait_ge(ss2_ready, 4 * TT)
            link(V.reduce_sum(ss2, ss2p, AX.X))
            V.tensor_scalar(rstd2, ss2, 1.0 / D, EPS, ALU.mult, ALU.add).then_inc(var2_ready, 1)
            dve.wait_ge(sd2_ready, 1)
            V.reciprocal(rstd2, rstd2).then_inc(rstd2_ready, 1)
            dve.wait_ge(rstd2_ready, 1)
            V.tensor_scalar(hn[:, 0, :], x_sb[:, 0, :], rstd2[:, 0:1], None, ALU.mult).then_inc(hn_ready, 1)
            dve.wait_ge(lg_filled, 1)
            dve.wait_ge(rbb_landed, 16)
            for t in range(TT):
                ins = V.scalar_tensor_tensor(out=lg[:, t, 0:N_E], in0=ps[:, 4 + t, 0:N_E],
                                             scalar=rstd2[:, t:t + 1], in1=rbb[:, :], op0=ALU.mult, op1=ALU.add)
            link(ins)
            for t in range(TT):
                ins = V.max(m8[:, t, :], lg[:, t, 0:N_E])
            link(ins)
            V.tensor_scalar(negm, m8[:, :, 0], -1.0, None, ALU.mult).then_inc(negm_ready, 1)
            link(V.tensor_copy(v8[:, :, 0:TOP_K], m8[:, :, 0:TOP_K]))
            for t in range(TT):
                ins = V.match_replace(rep[:, t, :], v8[:, t, :], lg[:, t, :], HIGH)
            link(ins)
            V.tensor_scalar(maskb[:, :, :], rep[:, :, 0:N_E], HIGH, None, ALU.is_equal).then_inc(mask_ready, 1)
            link(V.tensor_scalar(mask[:, :, :], rep[:, :, 0:N_E], HIGH, None, ALU.is_equal))
            dve.wait_ge(pos_filled, 1)
            V.scalar_tensor_tensor(out=pos[:, :, 0:N_E], in0=ps[:, 7, 0:2 * N_E].rearrange("p (t e) -> p t e", t=TT),
                                   scalar=1.0, in1=mask[:, :, :], op0=ALU.add, op1=ALU.mult).then_inc(pos_ready, 1)
            dve.wait_ge(pos_ready, 1)
            dve.wait_ge(iota_ready, 1)
            for t in range(TT):
                ins = V.tensor_scalar(sel0[:, t, :], iota[:, :], pos[:, t, 0:1], None, ALU.is_equal)
            ins.then_inc(sel0_ready, 1)
            link(V.reduce_max(cmax, ps[0:1, 7, 64:96], AX.X))
            V.tensor_copy(cnt_i[:, :], cmax).then_inc(count_ready, 1)
            dve.wait_ge(ex_ready, TT)
            link(V.tensor_tensor(ex[:, :, :], ex[:, :, :], mask[:, :, :], ALU.mult))
            for t in range(TT):
                ins = V.reduce_sum(gsum[:, t:t + 1], ex[:, t, :], AX.X)
            link(ins)
            link(V.reciprocal(rsum, gsum))
            for t in range(TT):
                V.tensor_scalar(gates[:, t, 0:N_E], ex[:, t, :], rsum[:, t:t + 1], None, ALU.mult)
                ins = V.tensor_scalar(gates4[:, t], ex[:, t, :].unsqueeze(1).to_broadcast([P, 4, N_E]),
                                      rsum[:, t:t + 1], None, ALU.mult)
            ins.then_inc(gates_ready, 1)

            def weigh(buf, e):
                for t in range(TT):
                    ins = V.tensor_scalar(sel_g[buf][:, t, :].rearrange("p (d s) -> p d s", d=2),
                                          iota[:, :].unsqueeze(1).to_broadcast([P, 2, SLOTS]),
                                          pos[:, t, ds(e, 1)], gates[:, t, ds(e, 1)], ALU.is_equal, ALU.mult)
                ins.then_inc(sel_ready, 1)

            def build(e, buf):
                V.tensor_copy(bsel[buf][:, :], ident3[:, ds(e, 1)].to_broadcast([96, SLOTS]))
                for t in range(TT):
                    V.tensor_scalar(sel[buf][:, t, :], iota[:, :], pos[:, t, ds(e, 1)], None, ALU.is_equal)
                weigh(buf, e)

            V.memset(stat[:, 30:31], 0.0).then_inc(gu_read, 1)

            def take_tokens():
                V.tensor_tensor(xg[:, :].rearrange("p (k s) -> p k s", k=KT),
                                ps[:, 6, :].rearrange("p (k s) -> p k s", k=KT),
                                vec[:, V_GFFN, :].unsqueeze(2).to_broadcast([P, KT, SLOTS]), ALU.mult).then_inc(
                    xg_ready, 1)

            for half in range(2):
                dve.wait_ge((gathered_half, gathered)[half], 1)
                V.tensor_tensor(xg[:, half * 256:(half + 1) * 256].rearrange("p (k s) -> p k s", k=4),
                                ps[:, 6 + half, 0:256].rearrange("p (k s) -> p k s", k=4),
                                vec[:, V_GFFN, 4 * half:4 * half + 4].unsqueeze(2).to_broadcast([P, 4, SLOTS]),
                                ALU.mult).then_inc((xg_half, xg_ready)[half], 1)
                if half == 0:
                    dve.wait_ge(gates_ready, 1)
                    weigh(0, 0)
            for t in range(TT):
                dve.wait_ge(part0_ready, t + 1)
                V.tensor_tensor(hn[:, t, :], hn[:, t, :], part[0][:, t, :], ALU.subtract).then_inc(rest_ready, 1)
            for t in range(TT):
                dve.wait_ge(part1_ready, t + 1)
                V.tensor_tensor(part[2][:, t, :], hn[:, t, :], part[1][:, t, :], ALU.subtract).then_inc(parts_ready, 1)
            dve.wait_ge(parts_ready, TT)

            def expert(E, X, e, par):
                build(e + (par + 1), 1 - par)
                dve.wait_ge(gu_used, KT * E + KT * (par + 1))
                V.tensor_scalar(g1[:, :], ps[:, 4, :], LIMIT, None, ALU.min).then_inc(glu_ready, 1)
                V.tensor_scalar(l1[:, :], ps[:, 5, :], LIMIT, -LIMIT, ALU.min, ALU.max).then_inc(gu_read, 1)
                dve.wait_ge(gu_read, E + (par + 2))
                V.scalar_tensor_tensor(out=l1[:, :], in0=l1[:, :], scalar=1.0, in1=g1[:, :], op0=ALU.add, op1=ALU.mult).then_inc(
                    t_ready, 1)
                dve.wait_ge(t_ready, E + (par + 1))
                dve.wait_ge(sig_ready, E + (par + 1))
                V.tensor_tensor(act_s[:, :], l1[:, :], act_s[:, :], ALU.mult).then_inc(act_ready, 1)
                dve.wait_ge(gathered, X + (par + 2))
                take_tokens()
                dve.wait_ge(actT_filled, E + (par + 1))
                V.tensor_copy(actT[:, :, :], ps[:, 7, :].rearrange("p (j s) -> p j s", j=4)).then_inc(actT_ready, 1)

            with dve.Fori(0, N_E // 2, 1) as i:
                for par in range(2):
                    expert(2 * i, 2 * i, 2 * i, par)

            def again(p):
                V.tensor_scalar(pos[:, :, :], pos[:, :, :], -float(SLOTS), None, ALU.add).then_inc(pos_ready, 1)
                dve.wait_ge(pos_ready, p + 1)
                build(0, 0)
                dve.wait_ge(gathered, PER_PASS * p + 1)
                take_tokens()
                with dve.Fori(0, N_E // 2, 1) as i:
                    for par in range(2):
                        expert(p * N_E + 2 * i, p * PER_PASS + 2 * i, 2 * i, par)

            overflow_passes(dve, again)
            dve.wait_ge(gfin_landed, 16)
            for t in range(TT):
                rsqrt_mean(ss3, rstd3, t, ss3_ready, var3_ready)
                reciprocal_of(rstd3, t, sd3_ready)
                V.scalar_tensor_tensor(out=fin[:, t, :].rearrange("p (h n) -> p h n", h=2),
                                       in0=ps[:, 2 * t:2 * t + 2, :], scalar=rstd3[:, t:t + 1],
                                       in1=gfin[:, :].rearrange("p (h n) -> p h n", h=2),
                                       op0=ALU.mult, op1=ALU.mult).then_inc(fin_ready, 1)


def kernel(**inputs):
    import concourse.bacc as bacc
    from concourse.bass_utils import run_bass_kernel_spmd as run

    a = {k: np.ascontiguousarray(v) for k, v in inputs.items()}
    rows = [a["norm_mix_g"][0], *a["conv_w"][0], a["conv_b"][0], a["lru_bx"][0], a["lru_ba"][0], a["lru_a_param"][0],
            a["norm_ffn_g"][0]]
    vecs = np.ascontiguousarray(np.stack(rows).reshape(N_VEC, KT, P).transpose(2, 0, 1).reshape(P, N_VEC * KT))
    half = ROPE // 2
    inv = (500000.0 ** (-np.arange(half, dtype=np.float32) * np.float32(2.0 / ROPE))).astype(np.float32)
    ang = (np.arange(T, dtype=np.float32)[None, :] * inv[:, None]).astype(np.float64)
    cos, sin = np.cos(ang), np.sin(ang)
    rope = np.stack([np.concatenate([cos, cos]), np.concatenate([-sin, sin])]).astype(np.float32)

    nc = bacc.Bacc("TRN2", target_bir_lowering=False, num_devices=1)
    named = {
        "x": a["x"], "vecs": vecs, "rope": rope, "w_in": a["w_in"], "lru_wx": a["lru_wx"], "lru_wa": a["lru_wa"],
        "w_proj_rnn": a["w_proj_rnn"], "w_proj_attn": a["w_proj_attn"], "w_out": a["w_out"],
        "router_w": a["router_w"], "router_b": a["router_b"],
        "w_gu": a["expert_w_gu"], "b_gu": a["expert_b_gu"], "w_down": a["expert_w_down"],
        "b_down": a["expert_b_down"], "norm_final_g": a["norm_final_g"],
    }
    arrays, args = {}, {}
    for name, v in named.items():
        arrays[f"in_{name}"] = v
        args[name] = nc.dram_tensor(f"in_{name}", v.shape, mybir.dt.from_np(v.dtype), kind="ExternalInput").ap()
    out = nc.dram_tensor("out_y", (1, T, D), mybir.dt.float32, kind="ExternalOutput").ap()
    program(nc, out=out, **args)
    return run(nc, [arrays], core_ids=[0]).results[0]["out_y"]
```
